# Optimizing a Trainium2 kernel written in Bass

```python
import math
import jax, jax.numpy as jnp
from jax import lax
import numpy as np

D_MODEL = 1024
BATCH = 1
SEQ = 256
DEPTH = 4

N_MIXERS = 3
HEAD_DIM = 64
PLE_DIM = 256
D_FF = 4 * D_MODEL
NORM_EPS = 1e-6
NEG_INF = -1e30
Q_BLOCK = 128

REL_BUCKETS = 32
REL_MAX_DIST = 128
REL_HEADS = D_MODEL // HEAD_DIM

DA_HEADS = D_MODEL // (2 * HEAD_DIM)
DA_IN = 3 * D_MODEL

NSA_HEADS = D_MODEL // HEAD_DIM
NSA_KV_GROUPS = 4
NSA_GROUP_SIZE = NSA_HEADS // NSA_KV_GROUPS
NSA_CMP_LEN = 32
NSA_CMP_STRIDE = 16
NSA_CMP_HIDDEN = 256
NSA_SEL_LEN = 64
NSA_TOP_N = 16
NSA_WINDOW = 512
NSA_Q_CHUNK = 64
NSA_FORCE_SCORE = 1e4
NSA_KV_DIM = NSA_KV_GROUPS * HEAD_DIM
NSA_IN = NSA_HEADS * HEAD_DIM + 6 * NSA_KV_DIM + 3 * NSA_HEADS

FOX_HEADS = D_MODEL // HEAD_DIM
FOX_IN = 3 * D_MODEL + FOX_HEADS

N_DA = (DEPTH + 2) // 3
N_NSA = (DEPTH + 1) // 3
N_FOX = DEPTH // 3


def rmsnorm(x, g):
    xf = x.astype(jnp.float32)
    y = xf * lax.rsqrt(jnp.mean(xf * xf, axis=-1, keepdims=True) + NORM_EPS)
    return (y * g.astype(jnp.float32)).astype(x.dtype)

def t5_bucket(dist):
    n = jnp.maximum(dist, 0)
    max_exact = REL_BUCKETS // 2
    nf = jnp.maximum(n, 1).astype(jnp.float32)
    large = max_exact + (jnp.log(nf / max_exact) / math.log(REL_MAX_DIST / max_exact)
                         * (REL_BUCKETS - max_exact)).astype(jnp.int32)
    large = jnp.minimum(large, REL_BUCKETS - 1)
    return jnp.where(n < max_exact, n, large)

def masked_softmax(s, mask):
    s = jnp.where(mask, s.astype(jnp.float32), NEG_INF)
    return jnp.where(mask, jax.nn.softmax(s, axis=-1), 0.0)

def query_blocks(a, blk):
    B, S = a.shape[:2]
    return jnp.moveaxis(a.reshape(B, S // blk, blk, *a.shape[2:]), 1, 0)

def merge_blocks(o):
    o = jnp.moveaxis(o, 0, 1)
    return o.reshape(o.shape[0], -1, *o.shape[3:])

def diff_attention(h, w_in, lam, subln_g, w_out, rel_bias, lam_init):
    B, S, _ = h.shape
    q, k, v = jnp.split(h @ w_in, 3, axis=-1)
    q = q.reshape(B, S, DA_HEADS, 2, HEAD_DIM)
    k = k.reshape(B, S, DA_HEADS, 2, HEAD_DIM)
    v = v.reshape(B, S, DA_HEADS, 2 * HEAD_DIM)
    lf = lam.astype(jnp.float32)
    lam_full = jnp.exp(jnp.sum(lf[0] * lf[1])) - jnp.exp(jnp.sum(lf[2] * lf[3])) + lam_init
    scale = HEAD_DIM ** -0.5
    key_pos = jnp.arange(S)

    def block(args):
        qb, q0 = args
        t = q0 + jnp.arange(Q_BLOCK)
        dist = t[:, None] - key_pos[None, :]
        mask = dist >= 0
        bias = rel_bias[t5_bucket(dist)].astype(jnp.float32)
        bias = jnp.moveaxis(bias, -1, 0).reshape(DA_HEADS, 2, Q_BLOCK, S)
        s = jnp.einsum('bqhcd,bkhcd->bhcqk', qb, k).astype(jnp.float32) * scale + bias[None]
        pr = masked_softmax(s, mask)
        a = pr[:, :, 0] - lam_full * pr[:, :, 1]
        return jnp.einsum('bhqk,bkhe->bqhe', a.astype(v.dtype), v)

    starts = jnp.arange(S // Q_BLOCK) * Q_BLOCK
    o = merge_blocks(lax.map(block, (query_blocks(q, Q_BLOCK), starts)))
    o = rmsnorm(o, subln_g) * (1.0 - lam_init)
    return o.reshape(B, S, D_MODEL) @ w_out

def nsa_attention(h, w_in, cmp_pe, cmp_w1, cmp_w2, w_out, rel_bias):
    B, S, _ = h.shape
    G, R, hd, Qc = NSA_KV_GROUPS, NSA_GROUP_SIZE, HEAD_DIM, NSA_Q_CHUNK
    proj = h @ w_in
    nq = NSA_HEADS * hd
    q = proj[..., :nq].reshape(B, S, G, R, hd)
    kv = proj[..., nq:nq + 6 * NSA_KV_DIM].reshape(B, S, 6, G, hd)
    k_cmp, v_cmp, k_sel, v_sel, k_win, v_win = [kv[:, :, i] for i in range(6)]
    gates = jax.nn.sigmoid(proj[..., nq + 6 * NSA_KV_DIM:].reshape(B, S, G, R, 3))
    scale = hd ** -0.5

    n_cmp = (S - NSA_CMP_LEN) // NSA_CMP_STRIDE + 1
    tok = jnp.arange(n_cmp)[:, None] * NSA_CMP_STRIDE + jnp.arange(NSA_CMP_LEN)[None, :]

    def compress(a, pe, w1, w2):
        blk = a[:, tok] + pe[None, None, :, None, :]
        blk = jnp.moveaxis(blk, 3, 2).reshape(B, n_cmp, G, NSA_CMP_LEN * hd)
        return jax.nn.gelu(blk @ w1) @ w2

    kc = compress(k_cmp, cmp_pe[0], cmp_w1[0], cmp_w2[0])
    vc = compress(v_cmp, cmp_pe[1], cmp_w1[1], cmp_w2[1])
    cmp_start = jnp.arange(n_cmp) * NSA_CMP_STRIDE
    cmp_end = cmp_start + NSA_CMP_LEN - 1

    n_sel_blk = S // NSA_SEL_LEN
    n_top = min(NSA_TOP_N, n_sel_blk)
    sel_start = jnp.arange(n_sel_blk) * NSA_SEL_LEN
    overlap = ((cmp_start[:, None] < sel_start[None, :] + NSA_SEL_LEN)
               & (cmp_end[:, None] >= sel_start[None, :])).astype(jnp.float32)
    ks_blk = jnp.moveaxis(k_sel.reshape(B, n_sel_blk, NSA_SEL_LEN, G, hd), 3, 1)
    vs_blk = jnp.moveaxis(v_sel.reshape(B, n_sel_blk, NSA_SEL_LEN, G, hd), 3, 1)

    pad = ((0, 0), (NSA_WINDOW, 0), (0, 0), (0, 0))
    kw_pad = jnp.pad(k_win, pad)
    vw_pad = jnp.pad(v_win, pad)

    rel = rel_bias.reshape(REL_BUCKETS, G, R)
    b_idx = jnp.arange(B)[:, None, None, None]
    g_idx = jnp.arange(G)[None, :, None, None]
    j_blk = jnp.arange(n_sel_blk)
    K_sel = n_top * NSA_SEL_LEN

    def chunk(args):
        qc, gc, q0 = args
        t = q0 + jnp.arange(Qc)
        d_c = t[:, None] - cmp_end[None, :]
        m_c = d_c >= 0
        b_c = jnp.moveaxis(rel[t5_bucket(d_c)], (2, 3), (0, 1)).astype(jnp.float32)
        s_c = jnp.einsum('bqgrd,bngd->bgrqn', qc, kc).astype(jnp.float32) * scale + b_c
        p_c = masked_softmax(s_c, m_c)
        o_c = jnp.einsum('bgrqn,bngd->bqgrd', p_c.astype(vc.dtype), vc)
        imp = jnp.einsum('bgrqn,nj->bgqj', p_c, overlap)
        cur = t // NSA_SEL_LEN
        forced = (j_blk[None, :] == 0) | (j_blk[None, :] == cur[:, None]) | (j_blk[None, :] == cur[:, None] - 1)
        valid = sel_start[None, :] <= t[:, None]
        imp = jnp.where(valid, jnp.where(forced, NSA_FORCE_SCORE, imp), -1.0)
        _, sel = lax.top_k(imp, n_top)
        k_g = ks_blk[b_idx, g_idx, sel].reshape(B, G, Qc, K_sel, hd)
        v_g = vs_blk[b_idx, g_idx, sel].reshape(B, G, Qc, K_sel, hd)
        pos = (sel[..., None] * NSA_SEL_LEN + jnp.arange(NSA_SEL_LEN)).reshape(B, G, Qc, K_sel)
        d_s = t[None, None, :, None] - pos
        m_s = (d_s >= 0)[:, :, None]
        b_s = jnp.moveaxis(rel[t5_bucket(d_s), g_idx], -1, 2).astype(jnp.float32)
        s_s = jnp.einsum('bqgrd,bgqkd->bgrqk', qc, k_g).astype(jnp.float32) * scale + b_s
        p_s = masked_softmax(s_s, m_s)
        o_s = jnp.einsum('bgrqk,bgqkd->bqgrd', p_s.astype(v_g.dtype), v_g)
        kw = lax.dynamic_slice_in_dim(kw_pad, q0, NSA_WINDOW + Qc, axis=1)
        vw = lax.dynamic_slice_in_dim(vw_pad, q0, NSA_WINDOW + Qc, axis=1)
        w_pos = q0 - NSA_WINDOW + jnp.arange(NSA_WINDOW + Qc)
        d_w = t[:, None] - w_pos[None, :]
        m_w = (d_w >= 0) & (d_w < NSA_WINDOW) & (w_pos[None, :] >= 0)
        b_w = jnp.moveaxis(rel[t5_bucket(d_w)], (2, 3), (0, 1)).astype(jnp.float32)
        s_w = jnp.einsum('bqgrd,bkgd->bgrqk', qc, kw).astype(jnp.float32) * scale + b_w
        p_w = masked_softmax(s_w, m_w)
        o_w = jnp.einsum('bgrqk,bkgd->bqgrd', p_w.astype(vw.dtype), vw)
        return gc[..., 0:1] * o_c + gc[..., 1:2] * o_s + gc[..., 2:3] * o_w

    starts = jnp.arange(S // Qc) * Qc
    o = merge_blocks(lax.map(chunk, (query_blocks(q, Qc), query_blocks(gates, Qc), starts)))
    return o.reshape(B, S, D_MODEL) @ w_out

def forgetting_attention(h, w_in, b_f, w_out):
    B, S, _ = h.shape
    proj = h @ w_in
    q = proj[..., :D_MODEL].reshape(B, S, FOX_HEADS, HEAD_DIM)
    k = proj[..., D_MODEL:2 * D_MODEL].reshape(B, S, FOX_HEADS, HEAD_DIM)
    v = proj[..., 2 * D_MODEL:3 * D_MODEL].reshape(B, S, FOX_HEADS, HEAD_DIM)
    log_f = jax.nn.log_sigmoid((proj[..., 3 * D_MODEL:] + b_f).astype(jnp.float32))
    c = jnp.cumsum(log_f, axis=1)
    c_k = jnp.moveaxis(c, 1, 2)
    scale = HEAD_DIM ** -0.5
    key_pos = jnp.arange(S)

    def block(args):
        qb, cq, q0 = args
        t = q0 + jnp.arange(Q_BLOCK)
        mask = t[:, None] >= key_pos[None, :]
        decay = jnp.moveaxis(cq, 1, 2)[..., None] - c_k[:, :, None, :]
        s = jnp.einsum('bqhd,bkhd->bhqk', qb, k).astype(jnp.float32) * scale + decay
        pr = masked_softmax(s, mask)
        return jnp.einsum('bhqk,bkhd->bqhd', pr.astype(v.dtype), v)

    starts = jnp.arange(S // Q_BLOCK) * Q_BLOCK
    o = merge_blocks(lax.map(block, (query_blocks(q, Q_BLOCK), query_blocks(c, Q_BLOCK), starts)))
    return o.reshape(B, S, D_MODEL) @ w_out

def sqrelu_mlp(h, w1, w2):
    return jnp.square(jax.nn.relu(h @ w1)) @ w2

def first_inputs(seed: int = 0) -> dict:
    key = jax.random.key(seed)
    ks = list(jax.random.split(key, 24))

    def nrm(i, shape, scale):
        return jax.random.normal(ks[i], shape, jnp.float32) * scale

    D = D_MODEL
    return {
        'x': nrm(0, (BATCH, SEQ, D), 1.0),
        'p': nrm(1, (DEPTH, BATCH, SEQ, PLE_DIM), 1.0),
        'rel_bias': nrm(2, (REL_BUCKETS, REL_HEADS), 0.5),
        'norm_g': 1.0 + nrm(3, (DEPTH, 4, D), 0.02),
        'mlp_w1': nrm(4, (DEPTH, D, D_FF), D ** -0.5),
        'mlp_w2': nrm(5, (DEPTH, D_FF, D), D_FF ** -0.5),
        'ple_w': nrm(6, (DEPTH, PLE_DIM, D), PLE_DIM ** -0.5),
        'ple_gate_w': nrm(7, (DEPTH, D, D), D ** -0.5),
        'da_w_in': nrm(8, (N_DA, D, DA_IN), D ** -0.5),
        'da_lambda': nrm(9, (N_DA, 4, HEAD_DIM), 0.1),
        'da_subln': 1.0 + nrm(10, (N_DA, 2 * HEAD_DIM), 0.02),
        'da_w_out': nrm(11, (N_DA, D, D), D ** -0.5),
        'nsa_w_in': nrm(12, (N_NSA, D, NSA_IN), D ** -0.5),
        'nsa_cmp_pe': nrm(13, (N_NSA, 2, NSA_CMP_LEN, HEAD_DIM), 0.1),
        'nsa_cmp_w1': nrm(14, (N_NSA, 2, NSA_CMP_LEN * HEAD_DIM, NSA_CMP_HIDDEN), (NSA_CMP_LEN * HEAD_DIM) ** -0.5),
        'nsa_cmp_w2': nrm(15, (N_NSA, 2, NSA_CMP_HIDDEN, HEAD_DIM), NSA_CMP_HIDDEN ** -0.5),
        'nsa_w_out': nrm(16, (N_NSA, D, D), D ** -0.5),
        'fox_w_in': nrm(17, (N_FOX, D, FOX_IN), D ** -0.5),
        'fox_b_f': 3.0 + nrm(18, (N_FOX, FOX_HEADS), 1.0),
        'fox_w_out': nrm(19, (N_FOX, D, D), D ** -0.5),
    }

def first_block(x, p, rel_bias, norm_g, mlp_w1, mlp_w2, ple_w, ple_gate_w,
              da_w_in, da_lambda, da_subln, da_w_out,
              nsa_w_in, nsa_cmp_pe, nsa_cmp_w1, nsa_cmp_w2, nsa_w_out,
              fox_w_in, fox_b_f, fox_w_out):
    ia, ib, ic = 0, 0, 0
    for i in range(DEPTH):
        g = norm_g[i]
        h = rmsnorm(x, g[0])
        kind = i % N_MIXERS
        if kind == 0:
            lam_init = 0.8 - 0.6 * math.exp(-0.3 * i)
            y = diff_attention(h, da_w_in[ia], da_lambda[ia], da_subln[ia], da_w_out[ia], rel_bias, lam_init)
            ia += 1
        elif kind == 1:
            y = nsa_attention(h, nsa_w_in[ib], nsa_cmp_pe[ib], nsa_cmp_w1[ib], nsa_cmp_w2[ib], nsa_w_out[ib], rel_bias)
            ib += 1
        else:
            y = forgetting_attention(h, fox_w_in[ic], fox_b_f[ic], fox_w_out[ic])
            ic += 1
        x = x + rmsnorm(y, g[1])
        y = sqrelu_mlp(rmsnorm(x, g[2]), mlp_w1[i], mlp_w2[i])
        x = x + rmsnorm(y, g[3])
        x = x + jax.nn.sigmoid(x @ ple_gate_w[i]) * (p[i] @ ple_w[i])
    return x


DEPTH_2 = 2

A_WIDTH = D_MODEL // 2
A_HEADS = A_WIDTH // HEAD_DIM
DILATED_BRANCHES = ((128, 1), (512, 4), (2048, 16))
BLOCK = 128
B_WIDTH = D_MODEL // 2
B_GROUPS = 4
B_GROUP_CH = B_WIDTH // B_GROUPS
CHUNK = 128
C_WIDTH = D_MODEL // 2
CONV_WIDTH = 31
D_WIDTH = D_MODEL // 2
D_HEADS = D_WIDTH // HEAD_DIM
N_BUCKETS = 32
MAX_DISTANCE = 2048
N_GROUPS = 4
EXPERTS_PER_GROUP = 4
N_EXPERTS = N_GROUPS * EXPERTS_PER_GROUP
EXPERT_TOP_K = 2
D_EXPERT = D_MODEL // 2
EPS = 1e-6
NEG = -1e30
N_EVEN = (DEPTH_2 + 1) // 2
N_ODD = DEPTH_2 // 2


def rms_norm(x, g):
    xf = x.astype(jnp.float32)
    y = xf * lax.rsqrt(jnp.mean(xf * xf, -1, keepdims=True) + EPS)
    return (y * g.astype(jnp.float32)).astype(x.dtype)

def layer_norm(x, g, b):
    xf = x.astype(jnp.float32)
    mu = jnp.mean(xf, -1, keepdims=True)
    xc = xf - mu
    var = jnp.mean(xc * xc, -1, keepdims=True)
    y = xc * lax.rsqrt(var + EPS) * g.astype(jnp.float32) + b.astype(jnp.float32)
    return y.astype(x.dtype)

def t5_bucket_2(dist):
    max_exact = N_BUCKETS // 2
    d = np.maximum(dist, 1).astype(np.float32)
    large = max_exact + (np.log(d / max_exact) / np.log(MAX_DISTANCE / max_exact)
                         * (N_BUCKETS - max_exact)).astype(np.int32)
    large = np.minimum(large, N_BUCKETS - 1)
    return np.where(dist < max_exact, dist, large).astype(np.int32)

def dilated_branch(q, k, v, rel_table, window, dilation):
    b, h, s, hd = q.shape
    n_keys = window // dilation
    sub_len = -(-s // dilation)
    lp = -(-sub_len // BLOCK) * BLOCK
    sp = lp * dilation
    nb = lp // BLOCK
    pad = ((0, 0), (0, 0), (0, sp - s), (0, 0))

    def to_blocks(t):
        t = jnp.pad(t, pad).reshape(b, h, lp, dilation, hd)
        t = jnp.swapaxes(t, 2, 3)
        return t.reshape(b, h, dilation, nb, BLOCK, hd)

    def with_prev(t):
        prev = jnp.pad(t, ((0, 0), (0, 0), (0, 0), (1, 0), (0, 0), (0, 0)))[:, :, :, :-1]
        return jnp.concatenate([prev, t], axis=4)

    qb = to_blocks(q)
    kb = with_prev(to_blocks(k))
    vb = with_prev(to_blocks(v))
    scores = jnp.einsum('bhrnqd,bhrnkd->bhrnqk', qb, kb)

    qi = np.arange(BLOCK)[:, None]
    kj = np.arange(2 * BLOCK)[None, :]
    sub_dist = qi + BLOCK - kj
    in_window = (sub_dist >= 0) & (sub_dist <= n_keys)
    bucket = t5_bucket_2(np.clip(sub_dist, 0, None) * dilation)
    bias = jnp.transpose(rel_table.astype(jnp.float32)[bucket], (2, 0, 1))
    first_block = (np.arange(nb) == 0)[:, None, None]
    valid = in_window[None] & ~(first_block & (kj < BLOCK)[None])
    logits = jnp.where(valid, scores + bias[None, :, None, None], NEG)

    mx = jnp.max(logits, -1)
    p = jnp.exp(logits - mx[..., None])
    den = jnp.sum(p, -1)
    num = jnp.einsum('bhrnqk,bhrnkd->bhrnqd', p, vb)

    def from_blocks(t):
        rest = t.shape[5:]
        t = t.reshape(b, h, dilation, lp, *rest)
        t = jnp.swapaxes(t, 2, 3).reshape(b, h, sp, *rest)
        return t[:, :, :s]

    return from_blocks(num), from_blocks(den), from_blocks(mx)

def dilated_attention(q, k, v, rel_table):
    b, s, h, hd = q.shape
    qf = jnp.swapaxes(q.astype(jnp.float32), 1, 2) * (hd ** -0.5)
    kf = jnp.swapaxes(k.astype(jnp.float32), 1, 2)
    vf = jnp.swapaxes(v.astype(jnp.float32), 1, 2)
    outs = [dilated_branch(qf, kf, vf, rel_table, w, d) for (w, d) in DILATED_BRANCHES]
    m_all = jnp.max(jnp.stack([m for (_, _, m) in outs]), 0)
    num = sum(n * jnp.exp(m - m_all)[..., None] for (n, _, m) in outs)
    den = sum(l * jnp.exp(m - m_all) for (_, l, m) in outs)
    o = num / den[..., None]
    return jnp.swapaxes(o, 1, 2).reshape(b, s, h * hd)

def spatial_gating(u, v, ln_g, ln_b, w_s, b_s):
    b, s, _ = v.shape
    u = jax.nn.gelu(u)
    v = layer_norm(jax.nn.gelu(v), ln_g, ln_b)
    vc = v.reshape(b, s // CHUNK, CHUNK, B_GROUPS, B_GROUP_CH)
    tril = np.tril(np.ones((CHUNK, CHUNK), dtype=bool))
    w = jnp.where(tril[None], w_s, 0.0)
    mixed = jnp.einsum('gts,bnsgc->bntgc', w, vc) + jnp.swapaxes(b_s, 0, 1)[None, None, :, :, None]
    return u * mixed.reshape(b, s, B_WIDTH).astype(u.dtype)

def conv_module(a, gate, w_dw, b_dw, ln_g, ln_b):
    hcur = a * jax.nn.sigmoid(gate)
    hcur = lax.conv_general_dilated(
        hcur, w_dw[:, None, :].astype(hcur.dtype), window_strides=(1,),
        padding=[(CONV_WIDTH - 1, 0)], dimension_numbers=('NWC', 'WIO', 'NWC'),
        feature_group_count=C_WIDTH) + b_dw
    hcur = layer_norm(hcur, ln_g, ln_b)
    return jax.nn.silu(hcur)

def stick_breaking_attention(q, k, v):
    b, s, h, hd = q.shape
    qf = jnp.transpose(q.astype(jnp.float32), (0, 2, 1, 3)) * (hd ** -0.5)
    kf = jnp.transpose(k.astype(jnp.float32), (0, 2, 1, 3))
    vf = jnp.transpose(v.astype(jnp.float32), (0, 2, 1, 3))
    nb = s // BLOCK
    q_blocks = jnp.moveaxis(qf.reshape(b, h, nb, BLOCK, hd), 2, 0)
    key_pos = jnp.arange(s)

    def block(args):
        qb, i = args
        z = jnp.einsum('bhqd,bhkd->bhqk', qb, kf)
        t = i * BLOCK + jnp.arange(BLOCK)
        causal = key_pos[None, :] < t[:, None]
        log_keep = jnp.where(causal, jax.nn.log_sigmoid(-z), 0.0)
        between = lax.cumsum(log_keep, axis=3, reverse=True) - log_keep
        att = jnp.where(causal, jnp.exp(jax.nn.log_sigmoid(z) + between), 0.0)
        return jnp.einsum('bhqk,bhkd->bhqd', att, vf)

    out = lax.map(block, (q_blocks, jnp.arange(nb)))
    out = jnp.moveaxis(out, 0, 2).reshape(b, h, s, hd)
    return jnp.transpose(out, (0, 2, 1, 3)).reshape(b, s, h * hd)

def hierarchical_moe(hin, w_group, b_group, w_router, b_router, w_gate, w_up, w_down):
    b, s, d = hin.shape
    xt = hin.reshape(b * s, d)
    xf = xt.astype(jnp.float32)
    g_prob = jax.nn.softmax(xf @ w_group.astype(jnp.float32) + b_group.astype(jnp.float32), -1)
    g_w, g_idx = lax.top_k(g_prob, 1)
    e_logits = jnp.einsum('td,gde->tge', xf, w_router.astype(jnp.float32)) + b_router.astype(jnp.float32)
    e_logits = jnp.take_along_axis(e_logits, g_idx[:, :, None], axis=1)[:, 0]
    e_val, e_idx = lax.top_k(e_logits, EXPERT_TOP_K)
    e_w = jax.nn.softmax(e_val, -1)
    flat_idx = g_idx * EXPERTS_PER_GROUP + e_idx
    gates = jnp.sum(jax.nn.one_hot(flat_idx, N_EXPERTS, dtype=jnp.float32)
                    * (g_w * e_w)[..., None], axis=1)
    y = jnp.zeros((b * s, d), jnp.float32)
    for e in range(N_EXPERTS):
        hid = jax.nn.silu(xt @ w_gate[e]) * (xt @ w_up[e])
        y = y + gates[:, e:e + 1] * (hid @ w_down[e]).astype(jnp.float32)
    return y.astype(hin.dtype).reshape(b, s, d)

def second_inputs(seed: int = 0) -> dict:
    key = jax.random.key(seed)
    ks = iter(jax.random.split(key, 32))

    def nrm(shape, scale):
        return scale * jax.random.normal(next(ks), shape, jnp.float32)

    d = D_MODEL
    ev_in = 3 * A_WIDTH + 2 * B_WIDTH
    od_in = 2 * C_WIDTH + 3 * D_WIDTH
    return {
        "x": nrm((BATCH, SEQ, d), 1.0),
        "c": nrm((BATCH, d), 1.0),
        "rel_bias": nrm((N_BUCKETS, A_HEADS), 0.5),
        "norm1_g": 1.0 + nrm((DEPTH_2, d), 0.1),
        "norm2_g": 1.0 + nrm((DEPTH_2, d), 0.1),
        "w_ada": nrm((DEPTH_2, d, 6 * d), 0.5 * d ** -0.5),
        "b_ada": nrm((DEPTH_2, 6 * d), 0.02),
        "ev_w_in": nrm((N_EVEN, d, ev_in), d ** -0.5),
        "ev_w_out": nrm((N_EVEN, A_WIDTH + B_WIDTH, d), (A_WIDTH + B_WIDTH) ** -0.5),
        "ev_gmlp_ln_g": 1.0 + nrm((N_EVEN, B_WIDTH), 0.1),
        "ev_gmlp_ln_b": nrm((N_EVEN, B_WIDTH), 0.02),
        "ev_w_s": nrm((N_EVEN, B_GROUPS, CHUNK, CHUNK), CHUNK ** -0.5),
        "ev_b_s": 1.0 + nrm((N_EVEN, B_GROUPS, CHUNK), 0.1),
        "od_w_in": nrm((N_ODD, d, od_in), d ** -0.5),
        "od_w_out": nrm((N_ODD, C_WIDTH + D_WIDTH, d), (C_WIDTH + D_WIDTH) ** -0.5),
        "od_w_dw": nrm((N_ODD, CONV_WIDTH, C_WIDTH), CONV_WIDTH ** -0.5),
        "od_b_dw": nrm((N_ODD, C_WIDTH), 0.02),
        "od_conv_ln_g": 1.0 + nrm((N_ODD, C_WIDTH), 0.1),
        "od_conv_ln_b": nrm((N_ODD, C_WIDTH), 0.02),
        "moe_w_group": nrm((DEPTH_2, d, N_GROUPS), d ** -0.5),
        "moe_b_group": nrm((DEPTH_2, N_GROUPS), 0.01),
        "moe_w_router": nrm((DEPTH_2, N_GROUPS, d, EXPERTS_PER_GROUP), d ** -0.5),
        "moe_b_router": nrm((DEPTH_2, N_GROUPS, EXPERTS_PER_GROUP), 0.01),
        "moe_w_gate": nrm((DEPTH_2, N_EXPERTS, d, D_EXPERT), d ** -0.5),
        "moe_w_up": nrm((DEPTH_2, N_EXPERTS, d, D_EXPERT), d ** -0.5),
        "moe_w_down": nrm((DEPTH_2, N_EXPERTS, D_EXPERT, d), D_EXPERT ** -0.5),
        "final_norm_g": 1.0 + nrm((d,), 0.1),
    }

def second_block(x, c, rel_bias, norm1_g, norm2_g, w_ada, b_ada, ev_w_in, ev_w_out,
              ev_gmlp_ln_g, ev_gmlp_ln_b, ev_w_s, ev_b_s, od_w_in, od_w_out, od_w_dw,
              od_b_dw, od_conv_ln_g, od_conv_ln_b, moe_w_group, moe_b_group, moe_w_router,
              moe_b_router, moe_w_gate, moe_w_up, moe_w_down, final_norm_g):
    b, s, _ = x.shape
    for layer in range(DEPTH_2):
        j = layer // 2
        mod = jax.nn.silu(c) @ w_ada[layer] + b_ada[layer]
        sh1, sc1, g1, sh2, sc2, g2 = jnp.split(mod[:, None, :], 6, axis=-1)
        hcur = rms_norm(x, norm1_g[layer]) * (1 + sc1) + sh1
        if layer % 2 == 0:
            proj = hcur @ ev_w_in[j]
            q, k, v, u, gv = jnp.split(
                proj, [A_WIDTH, 2 * A_WIDTH, 3 * A_WIDTH, 3 * A_WIDTH + B_WIDTH], axis=-1)
            o_a = dilated_attention(q.reshape(b, s, A_HEADS, HEAD_DIM),
                                    k.reshape(b, s, A_HEADS, HEAD_DIM),
                                    v.reshape(b, s, A_HEADS, HEAD_DIM), rel_bias)
            o_b = spatial_gating(u, gv, ev_gmlp_ln_g[j], ev_gmlp_ln_b[j], ev_w_s[j], ev_b_s[j])
            mix = jnp.concatenate([o_a.astype(x.dtype), o_b.astype(x.dtype)], -1) @ ev_w_out[j]
        else:
            proj = hcur @ od_w_in[j]
            a, gate, q, k, v = jnp.split(
                proj, [C_WIDTH, 2 * C_WIDTH, 2 * C_WIDTH + D_WIDTH, 2 * C_WIDTH + 2 * D_WIDTH], axis=-1)
            o_c = conv_module(a, gate, od_w_dw[j], od_b_dw[j], od_conv_ln_g[j], od_conv_ln_b[j])
            o_d = stick_breaking_attention(q.reshape(b, s, D_HEADS, HEAD_DIM),
                                           k.reshape(b, s, D_HEADS, HEAD_DIM),
                                           v.reshape(b, s, D_HEADS, HEAD_DIM))
            mix = jnp.concatenate([o_c.astype(x.dtype), o_d.astype(x.dtype)], -1) @ od_w_out[j]
        x = x + g1 * mix
        hcur = rms_norm(x, norm2_g[layer]) * (1 + sc2) + sh2
        x = x + g2 * hierarchical_moe(hcur, moe_w_group[layer], moe_b_group[layer],
                                      moe_w_router[layer], moe_b_router[layer],
                                      moe_w_gate[layer], moe_w_up[layer], moe_w_down[layer])
    return rms_norm(x, final_norm_g)


def setup_inputs(seed=0):
    out = dict(first_inputs(seed))
    for name, value in second_inputs(seed + 1).items():
        if name != "x":
            out[name + "_2"] = value
    return out


def reference(
    x, p, rel_bias, norm_g, mlp_w1, mlp_w2, ple_w, ple_gate_w, da_w_in, da_lambda, da_subln,
    da_w_out, nsa_w_in, nsa_cmp_pe, nsa_cmp_w1, nsa_cmp_w2, nsa_w_out, fox_w_in, fox_b_f,
    fox_w_out, c_2, rel_bias_2, norm1_g_2, norm2_g_2, w_ada_2, b_ada_2, ev_w_in_2, ev_w_out_2,
    ev_gmlp_ln_g_2, ev_gmlp_ln_b_2, ev_w_s_2, ev_b_s_2, od_w_in_2, od_w_out_2, od_w_dw_2,
    od_b_dw_2, od_conv_ln_g_2, od_conv_ln_b_2, moe_w_group_2, moe_b_group_2, moe_w_router_2,
    moe_b_router_2, moe_w_gate_2, moe_w_up_2, moe_w_down_2, final_norm_g_2,
):
    x = first_block(
        x, p, rel_bias, norm_g, mlp_w1, mlp_w2, ple_w, ple_gate_w, da_w_in, da_lambda, da_subln,
        da_w_out, nsa_w_in, nsa_cmp_pe, nsa_cmp_w1, nsa_cmp_w2, nsa_w_out, fox_w_in, fox_b_f,
        fox_w_out,
    )
    return second_block(
        x, c_2, rel_bias_2, norm1_g_2, norm2_g_2, w_ada_2, b_ada_2, ev_w_in_2, ev_w_out_2,
        ev_gmlp_ln_g_2, ev_gmlp_ln_b_2, ev_w_s_2, ev_b_s_2, od_w_in_2, od_w_out_2, od_w_dw_2,
        od_b_dw_2, od_conv_ln_g_2, od_conv_ln_b_2, moe_w_group_2, moe_b_group_2, moe_w_router_2,
        moe_b_router_2, moe_w_gate_2, moe_w_up_2, moe_w_down_2, final_norm_g_2,
    )


_drawn_inputs = setup_inputs


def setup_inputs(seed=0):
    import zlib

    import numpy as np

    out = dict(_drawn_inputs(seed))
    spreads = {}
    factors = {'da_subln': 2.967,
     'rel_bias_2': 8.0,
     'norm1_g_2': 4.989,
     'norm2_g_2': 4.582,
     'b_ada_2': 5.853,
     'ev_gmlp_ln_g_2': 8.0,
     'ev_gmlp_ln_b_2': 8.0,
     'ev_b_s_2': 8.0,
     'od_b_dw_2': 30.737,
     'od_conv_ln_g_2': 8.0,
     'od_conv_ln_b_2': 39.389,
     'moe_b_group_2': 8.0,
     'moe_b_router_2': 8.0}
    for name, (base, spread) in spreads.items():
        noise = np.random.default_rng([zlib.crc32(name.encode()), seed]).standard_normal(out[name].shape)
        drawn = base * np.exp(spread * noise) if base else spread * noise
        out[name] = __import__('jax').numpy.asarray(drawn.astype(out[name].dtype))
    for name, factor in factors.items():
        out[name] = (out[name] * factor).astype(out[name].dtype)
    return out
```

```python
import math
from collections import Counter
from contextlib import ExitStack

import numpy as np

import concourse.bass as bass
from concourse import mybir

F32 = mybir.dt.float32
BF16 = mybir.dt.bfloat16
ALU = mybir.AluOpType
ACT = mybir.ActivationFunctionType
AX = mybir.AxisListType

P = 128
D = 1024
KB = D // P
S = 256
DH = 64
FF = 4 * D
DEPTH, DEPTH2 = 4, 2
KINDS = ("da", "nsa", "fox", "da")
TILE = 4096
RING = 4
COLS = TILE // KB
NCMP = 15
NEXP = 16
CONVW = 31
NEG = -1e30
EPS = 1e-6
ROW = S + P
BIASH = 17
NADA = 48
ADAW = 256
ADA_PER = NADA // DEPTH
NTILES = 27 + 28 + 27 + 27 + 55 + 55


def bucket_first(dist):
    n = np.maximum(dist, 0)
    nf = np.maximum(n, 1).astype(np.float32)
    large = 16 + (np.log(nf / 16) / math.log(128 / 16) * 16).astype(np.int32)
    return np.where(n < 16, n, np.minimum(large, 31))


def bucket_second(dist):
    d = np.maximum(dist, 1).astype(np.float32)
    large = 16 + (np.log(d / 16) / np.log(2048 / 16) * 16).astype(np.int32)
    return np.where(dist < 16, dist, np.minimum(large, 31))


def branch_count(d):
    return np.where(d < 0, 0, (d <= 128).astype(int) + (d % 4 == 0) + (d % 16 == 0))


def one_hot_rows(bucket, dist, open_):
    out = np.zeros((P, len(dist)), np.float32)
    for j, d in enumerate(dist):
        if open_[j]:
            out[int(bucket(np.array(d))), j] = 1
        else:
            out[32, j] = NEG
    return out


def first_head(j, half):
    return 4 * (2 * (j // 4) + half) + j % 4


def resident_layout():
    widths = [
        ("ident", 128), ("mean1024", 128), ("mean128", 128), ("mean512", 128), ("ones", 128),
        ("later", 128), ("tri", 128), ("strict", ROW), ("cnt", ROW), ("rowmask", 1), ("rank", 4),
        ("eps", 1), ("norm_g", 4 * 4 * 8), ("norm1_g2", 16), ("norm2_g2", 16), ("final_g2", 8),
        ("c2", 8), ("b_ada", 96), ("subln", 2), ("dw", 4 * CONVW), ("dwb", 4), ("convg", 4),
        ("convb", 4), ("nsa_gate", 8 * 48), ("cmp_w2k", 2 * 128), ("cmp_w2v", 2 * 64), ("pe", 32),
        ("fox_wf", 8 * 16), ("fox_bf", 1), ("router", 2 * 8 * 20), ("router_b", 40), ("gmlp_bs", 512),
    ]
    at, out = 0, {}
    for name, w in widths:
        out[name] = (at, at + w)
        at += w
    return out, at


RES, RES_W = resident_layout()
SETUP = {"oh1": (0, 384), "oh2": (384, 768), "ohf": (768, 1280), "rel1": (1280, 1297),
         "rel2": (1297, 1305), "lam": (1305, 1817), "w_s": (1817, 2329)}
SETUP_W = 2329


class Stage:

    def __init__(self, kind, layer, at):
        self.kind, self.layer, self.at = kind, layer, at


def schedule():
    n, out = Counter(), []

    def add(kind, layer=0, **uses):
        out.append(Stage(kind, layer, Counter(n)))
        n.update(uses)

    add("setup", unit=4)
    for i in range(DEPTH):
        kind = KINDS[i]
        add("norm", i, unit=1, sq=1, h=1, rstd=1)
        if kind == "da":
            add("da", i, unit=12 + 16 + 4, tile=6, head=8, item=16, tr=8, pv=8, sq=1, sub=4, o=1)
        elif kind == "nsa":
            add("nsa", i, unit=10 + 1 + 4 + 32, tile=7, head=16, item=32, tr=32, pv=16)
        else:
            add("fox", i, unit=12 + 1 + 16, tile=6, head=16, item=16, tr=16, pv=16)
        add("outproj", i, tile=2, acc=1)
        add("postnorm", i, unit=1, sq=1, rstd=1, x=1)
        add("norm", i, unit=1, sq=1, h=1, rstd=1)
        add("mlp", i, unit=16 + 1, tile=16, acc=1, ada=1)
        add("postnorm", i, unit=1 + 4, tile=1, sq=1, rstd=1, x=1)
        add("ple", i, unit=4, tile=2, x=1)
    for i in range(DEPTH2):
        add("norm2", i, unit=1, sq=1, h=1, rstd=1)
        if i == 0:
            add("ev", i, unit=10 + 8 + 2, tile=5, head=8, item=8, tr=8, pv=8)
        else:
            add("od", i, unit=10 + 8 + 2, tile=5, head=8, item=8, tr=8, pv=8, sq=1, rstd=1, o=1)
        add("outproj", i, tile=2, acc=1)
        add("residual", i, x=1)
        add("norm2", i, unit=1, sq=1, h=1, rstd=1)
        add("moe", i, unit=1 + 1 + 8 + 64, tile=48, acc=1)
        add("residual", i, x=1)
    add("final", 0, unit=1, sq=1, rstd=1)
    for st, after in zip(out, out[1:]):
        st.embeds = after.kind == "ple"
    assert n["tile"] == NTILES, n["tile"]
    return out, n


def build(nc, x_in, resident, setup, gmlp_gb, stream, ada_stream, out, stages=None):
    plan, total = schedule()
    n_tiles = NTILES
    if stages is not None:
        n_tiles, n_x = plan[stages].at["tile"], plan[stages].at["x"]
        plan = plan[:stages]
    last = plan[-1]
    with ExitStack() as ctx:
        def sb(name, shape, dt=F32):
            return ctx.enter_context(nc.sbuf_tensor(name, shape, dt))

        def sem(name):
            return ctx.enter_context(nc.semaphore(name))

        ring = sb("weight_ring", [P, RING, TILE])
        ada_ring = sb("ada_ring", [P, 2, KB * ADAW])
        xT = sb("xT", [P, KB * S])
        hT = sb("hT", [P, KB * S])
        oT = sb("oT", [P, KB * S])
        big = sb("big", [P, 32 * S])
        att = sb("att", [P, 4096])
        biasT = sb("bias", [P, BIASH * ROW])
        res = sb("resident", [P, RES_W])
        cmp_bias = sb("cmp_bias", [P, 2 * NCMP * 16])
        wsT = sb("wsT", [P, 512])
        lnv = sb("lnv", [P, S])
        rstd = sb("rstd", [P, S])
        stat_max = sb("stat_max", [P, 16 * 6])
        stat_sum = sb("stat_sum", [P, 16 * 6])
        stat_coef = sb("stat_coef", [P, 16 * 6])
        lamv = sb("lamv", [P, 16])
        gates_sb = sb("gates_sb", [P, 2 * 48])
        gel = sb("gel", [P, 2 * 120])
        kcT = sb("kcT", [P, 60])
        vc = sb("vc", [16, 256])
        fox_f = big[0:16, 24 * S:28 * S]
        mod = sb("mod", [P, 96])
        gain2 = sb("gain2", [P, 32])
        silu_c = sb("silu_c", [P, 8])
        zeros = sb("zeros", [1, 512], BF16)
        rt = sb("routing", [P, 320])
        gateT = lnv[0:16, :]
        acc = ctx.enter_context(nc.psum_tensor("acc", [P, 4, 512], F32))
        work = ctx.enter_context(nc.psum_tensor("work", [P, 4, 512], F32))
        rows1 = nc.dram_tensor("bias_rows1", (BIASH, ROW), F32, kind="Internal").ap()
        rows2 = nc.dram_tensor("bias_rows2", (8, ROW), F32, kind="Internal").ap()
        copies1 = nc.dram_tensor("bias_copies1", (BIASH, P, ROW), F32, kind="Internal").ap()
        copies2 = nc.dram_tensor("bias_copies2", (8, P, ROW), F32, kind="Internal").ap()

        landed = [sem(f"tile_landed{i}") for i in range(RING)]
        tile_begun = sem("tile_begun")
        ada_landed = [sem(f"ada_landed{i}") for i in range(2)]
        ada_step = sem("ada_step")
        work_full = sem("work_full")
        evac = [sem(f"evacuated{i}") for i in range(4)]
        acc_full = sem("acc_full")
        sq_ready = sem("squares_ready")
        rstd_ready = sem("rstd_ready")
        sub_rstd = sem("sub_rstd_ready")
        h_ready = sem("h_ready")
        x_ready = sem("x_ready")
        o_ready = sem("o_ready")
        logits_ready = sem("logits_ready")
        exps_done = sem("exps_done")
        probs_ready = sem("probs_ready")
        tr_full = sem("transposed_full")
        tr_free = sem("transposed_out")
        pv_full = sem("pv_full")
        pv_free = sem("pv_out")
        act_step = sem("act_step")
        dve_step = sem("dve_step")
        loads = sem("loads")
        x_loaded = sem("x_loaded")
        rows_out = sem("bias_rows_out")
        bias_in = sem("bias_in")
        bias2_in = sem("bias2_in")
        mlp_step = sem("mlp_step")
        z_ready = sem("z_ready")
        soft_ready = sem("soft_ready")
        keep_ready = sem("keep_ready")
        gated = sem("silu_gated")
        route_a = sem("route_asks")
        route_b = sem("route_exps")
        gates_ready = sem("gates_ready")
        gates_out = sem("gateT_ready")
        setup_done = sem("setup_done")
        cum_ready = sem("cum_ready")
        conv_done = sem("conv_done")
        mod_ready = sem("mod_ready")
        stored = sem("stored")

        def R(name, a=0, b=None, rows=slice(0, P)):
            lo, hi = RES[name]
            return res[rows, lo + a:(hi if b is None else lo + b)]

        def SU(name, a=0, b=None, rows=slice(0, P)):
            lo, hi = SETUP[name]
            return big[rows, lo + a:(hi if b is None else lo + b)]

        def blk(t, k, n=1, rows=slice(0, P)):
            return t[rows, k * S:(k + n) * S]

        def wk(u, a=0, b=512, rows=slice(0, P)):
            return work[rows, u % 4, a:b]

        def accb(m, rows=slice(0, P)):
            return acc[rows, m // 2, (m % 2) * S:(m % 2 + 1) * S]

        def wtile(t, k, c0, n=P, width=COLS):
            return ring[:, t % RING, k * width + c0:k * width + c0 + n]

        def prob(slot, a, b):
            return att[:, slot * 512 + a:slot * 512 + b]

        def ptr(slot, a, b, rows=slice(0, P)):
            return att[rows, 2048 + slot * 1024 + a:2048 + slot * 1024 + b]

        def half(h):
            return slice(64 * h, 64 * h + 64)

        def bias_of(h, a=0, b=ROW):
            return biasT[:, h * ROW + a:h * ROW + b]

        def stat(t, h, a, b):
            return t[:, 6 * h + a:6 * h + b]

        SQ = 24
        V0 = {"da": 16, "nsa": 16, "fox": 16, "ev": 8, "od": 8}

        def wait_evacuated(eng, units):
            for u in sorted(units)[-4:]:
                eng.wait_ge(evac[u % 4], u // 4 + 1)

        def wait_x(eng, st, quarter=3):
            if st.at["x"] == 0:
                eng.wait_ge(x_loaded, 16)
            else:
                eng.wait_ge(x_ready, 4 * (st.at["x"] - 1) + quarter + 1)

        def pe_open(pe, u):
            if u >= 4:
                pe.wait_ge(evac[u % 4], u // 4)

        def pe_tile(pe, t):
            pe.wait_ge(landed[t % RING], 16 * (t // RING + 1))

        def mm(pe, o, a, b, start=True, stop=True):
            return pe.matmul(o, a, b, start=start, stop=stop, skip_group_check=True)

        def pe_feature_tile(pe, t, units, rhs, wait_k=None, out_of=None):
            pe_tile(pe, t)
            for m in range(4):
                if out_of is None and m % 2 == 0:
                    pe_open(pe, units[m // 2])
                o = wk(units[m // 2], (m % 2) * S, (m % 2 + 1) * S) if out_of is None else out_of(m)
                for k in range(KB):
                    if wait_k is not None and m == 0:
                        wait_k(k)
                    ins = mm(pe, o, wtile(t, k, m * P), rhs(k), k == 0, k == KB - 1)
                    if m == 0 and k == 0:
                        ins.then_inc(tile_begun, 1)
                if out_of is None and m % 2 == 1:
                    ins.then_inc(work_full, 1)
            return ins

        def pe_token_tile(pe, t, units):
            pe_tile(pe, t)
            for tt in range(2):
                pe_open(pe, units[tt])
                for k in range(KB):
                    ins = mm(pe, wk(units[tt]), hT[:, k * S + tt * P:k * S + tt * P + P],
                             wtile(t, k, 0, COLS), k == 0, k == KB - 1)
                    if tt == 0 and k == 0:
                        ins.then_inc(tile_begun, 1)
                ins.then_inc(work_full, 1)

        def pe_means(pe, u, sq, mean, blocks=KB):
            pe_open(pe, u)
            for k in range(blocks):
                if k * 4 % blocks == 0:
                    pe.wait_ge(sq_ready, 4 * sq + k * 4 // blocks + 1)
                ins = mm(pe, wk(u, 0, S), mean, blk(big, SQ + k), k == 0, k == blocks - 1)
            ins.then_inc(work_full, 1)

        def pe_project(pe, st, forms):
            for j, form in enumerate(forms):
                t, u = st.at["tile"] + j, st.at["unit"] + 2 * j
                if form == "F":
                    first = (lambda k: pe.wait_ge(h_ready, 8 * (st.at["h"] - 1) + k + 1)) if j == 0 else None
                    pe_feature_tile(pe, t, (u, u + 1), lambda k: blk(hT, k), first)
                else:
                    pe_token_tile(pe, t, (u, u + 1))

        def pe_transpose(pe, o, a, n=P):
            return pe.transpose(o, a, R("ident", 0, n, rows=slice(0, n)))

        def pe_norm(pe, st):
            pe_means(pe, st.at["unit"], st.at["sq"], R("mean1024"))

        def pe_setup(pe, st):
            pe.wait_ge(loads, 16 * 2)
            pe.wait_ge(dve_step, 1)
            k33 = slice(0, 33)
            mm(pe, wk(0, 0, ROW, slice(0, BIASH)), SU("rel1", rows=k33), SU("oh1", rows=k33)).then_inc(work_full, 1)
            mm(pe, wk(1, 0, ROW, slice(0, 8)), SU("rel2", rows=k33), SU("oh2", rows=k33)).then_inc(work_full, 1)
            for tt in range(2):
                for n in range(NCMP):
                    d0 = 256 + tt * P - 16 * n - 31
                    ins = mm(pe, wk(2, (tt * NCMP + n) * 16, (tt * NCMP + n) * 16 + 16),
                             SU("ohf", d0, d0 + P, k33), SU("rel1", 0, 16, k33))
            ins.then_inc(work_full, 1)
            for g in range(4):
                ins = pe_transpose(pe, wk(3, g * P, g * P + P), SU("w_s", g * P, g * P + P))
            ins.then_inc(work_full, 1)

        def ahead(s, heads, by):
            return [n for n in (range(by + 1) if s == 0 else (s + by,)) if n < heads]

        def pe_scores(pe, u, q, k, rows, opened=True):
            if opened:
                pe_open(pe, u)
            qa, ka = blk(big, q, rows=rows), blk(big, k, rows=rows)
            mm(pe, wk(u, 0, P), qa[:, 0:P], ka[:, 0:P])
            return mm(pe, wk(u, P, ROW), qa[:, P:S], ka[:, 0:S])

        def pe_turn(pe, f, slot, extra=None):
            if f >= 2:
                pe.wait_ge(tr_free, f - 1)
            o = acc[:, f % 2, :]
            pe_transpose(pe, o[:, 0:P], prob(slot, 0, P))
            pe_transpose(pe, o[:, P:2 * P], prob(slot, P, 2 * P))
            ins = pe_transpose(pe, o[:, 2 * P:3 * P], prob(slot, 2 * P, 3 * P))
            if extra is not None:
                ins = pe_transpose(pe, acc[0:NCMP, f % 2, ROW:512], extra)
            ins.then_inc(tr_full, 1)

        def pe_pv(pe, n, rows, parts):
            if n >= 2:
                pe.wait_ge(pv_free, n - 1)
            for i, (v, pr, a, b) in enumerate(parts):
                ins = mm(pe, acc[rows, 2 + n % 2, a:b], v, pr, i == 0, i == len(parts) - 1)
            ins.then_inc(pv_full, 1)

        def pe_value(v0, tt, c, n, width=4):
            return big[:, v0 * S + tt * width * S + c:v0 * S + tt * width * S + c + n]

        def pe_da(pe, st):
            pe_project(pe, st, "FFFFTT")
            u0, tr0, pv0, pr0 = st.at["unit"] + 12, st.at["tr"], st.at["pv"], st.at["head"]
            wait_evacuated(pe, range(u0 - 4, u0))
            for s in range(8 + 2):
                for n in ahead(s, 8, 1):
                    for c in range(2):
                        pe_scores(pe, u0 + 2 * n + c, n, 8 + n, half(c)).then_inc(work_full, 1)
                if 0 <= s - 1 < 8:
                    h = s - 1
                    pe.wait_ge(probs_ready, pr0 + h + 1)
                    pe_turn(pe, tr0 + h, 2 * (h % 2))
                if 0 <= s - 2 < 8:
                    h = s - 2
                    pe.wait_ge(tr_free, tr0 + h + 1)
                    pe_pv(pe, pv0 + h, slice(0, P), [
                        (pe_value(16, 0, h * P, P), ptr(h % 2, 0, S), 0, S),
                        (pe_value(16, 1, h * P, P), ptr(h % 2, S, ROW), P, S)])
            for q in range(4):
                u = u0 + 16 + q
                pe_open(pe, u)
                pe.wait_ge(sq_ready, 4 * st.at["sq"] + q + 1)
                mm(pe, wk(u), R("mean128"), blk(big, SQ + 2 * q, 2)).then_inc(work_full, 1)

        def pe_nsa(pe, st):
            pe_project(pe, st, "FFFFT")
            ug = st.at["unit"] + 10
            pe_open(pe, ug)
            for tt in range(2):
                for k in range(KB):
                    ins = mm(pe, wk(ug, tt * 48, tt * 48 + 48), hT[:, k * S + tt * P:k * S + tt * P + P],
                             R("nsa_gate", k * 48, k * 48 + 48), k == 0, k == KB - 1)
            ins.then_inc(work_full, 1)
            z0 = 20 * S
            for kv in range(2):
                t, u = st.at["tile"] + 5 + kv, ug + 1 + kv
                pe_tile(pe, t)
                pe_open(pe, u)
                pe.wait_ge(z_ready, kv + 1)
                for m in range(2):
                    for j in range(16):
                        ins = mm(pe, wk(u, m * 60, m * 60 + 60), wtile(t, j, m * P, P, 256),
                                 big[:, z0 + kv * 960 + j * 60:z0 + kv * 960 + j * 60 + 60], j == 0, j == 15)
                        if m == 0 and j == 0:
                            ins.then_inc(tile_begun, 1)
                ins.then_inc(work_full, 1)
            u = ug + 3
            pe_open(pe, u)
            wait_evacuated(pe, [ug + 1])
            for m in range(2):
                ins = mm(pe, wk(u, 0, 60), R("cmp_w2k", m * P, m * P + P), gel[:, m * 60:m * 60 + 60], m == 0, m == 1)
            ins.then_inc(work_full, 1)
            u = ug + 4
            pe_open(pe, u)
            wait_evacuated(pe, [ug + 2])
            for g in range(4):
                for m in range(2):
                    ins = mm(pe, wk(u, g * DH, g * DH + DH, slice(0, NCMP)),
                             gel[:, 120 + m * 60 + g * NCMP:120 + m * 60 + g * NCMP + NCMP],
                             R("cmp_w2v", m * DH, m * DH + DH), m == 0, m == 1)
            ins.then_inc(work_full, 1)
            u0, tr0, pv0, pr0 = ug + 5, st.at["tr"], st.at["pv"], st.at["head"]
            wait_evacuated(pe, range(u0 - 4, u0))
            for s in range(16 + 2):
                for n in ahead(s, 16, 1):
                    j, hf = n // 2, n % 2
                    g = 2 * (j // 4) + hf
                    u = u0 + 2 * n
                    pe_scores(pe, u, j, 12 + g // 2, half(hf))
                    for tt in range(2):
                        ins = mm(pe, wk(u, ROW + 16 * tt, ROW + 16 * tt + NCMP),
                                 big[half(hf), j * S + tt * P:j * S + tt * P + P],
                                 kcT[half(hf), g * NCMP:g * NCMP + NCMP])
                    ins.then_inc(work_full, 1)
                    pe_scores(pe, u + 1, j, 14 + g // 2, half(hf)).then_inc(work_full, 1)
                if 0 <= s - 1 < 16:
                    h = s - 1
                    pe.wait_ge(probs_ready, pr0 + h + 1)
                    for c in range(2):
                        pe_turn(pe, tr0 + 2 * h + c, 2 * (h % 2) + c,
                                prob(2 * (h % 2), ROW + 16 * c, ROW + 16 * c + NCMP))
                if 0 <= s - 2 < 16:
                    h = s - 2
                    g = 2 * (h // 8) + h % 2
                    pe.wait_ge(tr_free, tr0 + 2 * h + 2)
                    n15, vcg = slice(0, NCMP), vc[0:NCMP, g * DH:g * DH + DH]
                    parts = []
                    for c in range(2):
                        for tt in range(2):
                            parts.append((pe_value(16, tt, c * 256 + g * DH, DH, 2),
                                          ptr(h % 2, 512 * c + S * tt, 512 * c + S + P * tt), P * tt, S))
                    parts.append((vcg, ptr(h % 2, ROW, 512, n15), 0, P))
                    parts.append((vcg, ptr(h % 2, 512 + ROW, 1024, n15), P, S))
                    pe_pv(pe, pv0 + h, half(h % 2), parts)

        def pe_heads(pe, st, u0, heads, k0, v0, width, after=None, decay=False):
            tr0, pv0, pr0 = st.at["tr"], st.at["pv"], st.at["head"]
            for s in range(heads + 2):
                for n in ahead(s, heads, 2):
                    u, j, hf = u0 + n, n // 2, half(n % 2)
                    pe_open(pe, u)
                    spans = ((0, P, 0, P), (P, ROW, P, S))
                    for a, b, q, keys in spans:
                        ins = mm(pe, wk(u, a, b), blk(big, j, rows=hf)[:, q:q + P],
                                 blk(big, k0 + j, rows=hf)[:, 0:keys], True, not decay)
                        if decay:
                            one = R("ident", n, n + 1, slice(0, 16))
                            mm(pe, wk(u, a, b), one.broadcast_to([16, P]), fox_f[:, 3 * S:3 * S + keys], False, False)
                            ins = mm(pe, wk(u, a, b), fox_f[:, 2 * S + q:2 * S + q + P],
                                     one.broadcast_to([16, keys]), False, True)
                    ins.then_inc(work_full, 1)
                if 0 <= s - 1 < heads:
                    h = s - 1
                    pe.wait_ge(probs_ready, pr0 + h + 1)
                    pe_turn(pe, tr0 + h, h % 4)
                if 0 <= s - 2 < heads:
                    h = s - 2
                    pe.wait_ge(tr_free, tr0 + h + 1)
                    pe_pv(pe, pv0 + h, half(h % 2), [
                        (pe_value(v0, 0, h * DH, DH, width), ptr(h % 2, 0, S), 0, S),
                        (pe_value(v0, 1, h * DH, DH, width), ptr(h % 2, S, ROW), P, S)])

        def pe_fox(pe, st):
            pe_project(pe, st, "FFFFTT")
            u = st.at["unit"] + 12
            pe_open(pe, u)
            for k in range(KB):
                ins = mm(pe, wk(u, 0, S, slice(0, 16)), R("fox_wf", k * 16, k * 16 + 16), blk(hT, k), k == 0, k == KB - 1)
            ins.then_inc(work_full, 1)
            wait_evacuated(pe, range(u - 4, u))
            pe.wait_ge(cum_ready, 1)
            pe_heads(pe, st, u + 1, 16, 8, 16, 4, decay=True)

        def pe_ev(pe, st):
            pe_project(pe, st, "FFTFT")
            u0 = st.at["unit"] + 10
            wait_evacuated(pe, range(u0 - 4, u0))
            pe_heads(pe, st, u0, 8, 4, 8, 2)
            pe.wait_ge(z_ready, 3)
            for i in range(2):
                u = u0 + 8 + i
                pe_open(pe, u)
                for g in (2 * i, 2 * i + 1):
                    for n in range(2):
                        o = wk(u, (g % 2) * S + n * P, (g % 2) * S + n * P + P)
                        mm(pe, o, big[:, 16 * S + n * 512 + g * P:16 * S + n * 512 + g * P + P],
                           wsT[:, g * P:g * P + P], True, False)
                        ins = mm(pe, o, R("ones", rows=slice(0, 1)), R("gmlp_bs", g * P, g * P + P, slice(0, 1)), False, True)
                ins.then_inc(work_full, 1)

        def pe_od(pe, st):
            pe_project(pe, st, "FFFFT")
            u0, tr0, pv0, pr0 = st.at["unit"] + 10, st.at["tr"], st.at["pv"], st.at["head"]
            wait_evacuated(pe, range(u0 - 4, u0))
            for s in range(8 + 2):
                for n in ahead(s, 8, 1):
                    u, j, hf = u0 + n, n // 2, half(n % 2)
                    pe_open(pe, u)
                    qa, ka = blk(big, j, rows=hf), blk(big, 4 + j, rows=hf)
                    mm(pe, wk(u, 0, S), ka[:, 0:P], qa[:, 0:S])
                    mm(pe, wk(u, S, ROW), ka[:, P:S], qa[:, P:S]).then_inc(work_full, 1)
                if 0 <= s - 1 < 8:
                    h = s - 1
                    pe.wait_ge(keep_ready, h + 1)
                    if h < 2:
                        pe.wait_ge(tr_free, tr0)
                    o, keep = acc[:, (tr0 + h) % 2, :], 2 * (h % 2) + 1
                    mm(pe, o[:, 0:S], R("later"), prob(keep, 0, S), True, False)
                    mm(pe, o[:, P:S], R("ones"), prob(keep, S, ROW), False, True)
                    mm(pe, o[:, S:ROW], R("later"), prob(keep, S, ROW)).then_inc(tr_full, 1)
                if 0 <= s - 2 < 8:
                    h = s - 2
                    pe.wait_ge(probs_ready, pr0 + h + 1)
                    pe_pv(pe, pv0 + h, half(h % 2), [
                        (pe_value(8, 0, h * DH, DH, 2), ptr(h % 2, 0, S), 0, S),
                        (pe_value(8, 1, h * DH, DH, 2), ptr(h % 2, S, ROW), P, S)])
            u = u0 + 8
            pe.wait_ge(conv_done, 1)
            pe_open(pe, u)
            for k in range(4):
                ins = mm(pe, wk(u, 0, S), R("mean512"), blk(big, 17 + k), k == 0, k == 3)
            ins.then_inc(work_full, 1)
            pe_means(pe, u + 1, st.at["sq"], R("mean512"), 4)

        def pe_outproj(pe, st, prev):
            pe.wait_ge(pv_free, st.at["pv"])
            if prev.kind in ("da", "od"):
                pe.wait_ge(o_ready, st.at["o"])
            if prev.kind == "ev":
                wait_evacuated(pe, [st.at["unit"] - 2, st.at["unit"] - 1])
            for j in range(2):
                ins = pe_feature_tile(pe, st.at["tile"] + j, None, lambda k: blk(oT, k),
                                      out_of=lambda m, j=j: accb(4 * j + m))
            ins.then_inc(acc_full, 1)

        def pe_clear_acc(pe):
            for b in range(4):
                mm(pe, acc[:, b, :], zeros[0:1, 0:P], zeros[0:1, :])

        def pe_mlp(pe, st):
            u0, t0 = st.at["unit"], st.at["tile"]
            with pe.Fori(0, 2) as i:
                for j in range(4):
                    t = t0 + j
                    pe.wait_ge(landed[t % RING], i * 16 + 16 * (t // RING + 1))
                    for m in range(4):
                        u = u0 + 2 * j + m // 2
                        if m % 2 == 0:
                            pe.wait_ge(evac[u % 4], i * 2 + u // 4)
                        for k in range(KB):
                            if j == 0 and m == 0:
                                pe.wait_ge(h_ready, 8 * (st.at["h"] - 1) + k + 1)
                            ins = mm(pe, wk(u, (m % 2) * S, (m % 2 + 1) * S), wtile(t, k, m * P), blk(hT, k),
                                     k == 0, k == KB - 1)
                            if m == 0 and k == 0:
                                ins.then_inc(tile_begun, 1)
                        if m % 2 == 1:
                            ins.then_inc(work_full, 1)
            pe_clear_acc(pe)
            with pe.Fori(0, 2) as i:
                for j in range(4):
                    t = t0 + 8 + j
                    pe.wait_ge(landed[t % RING], i * 16 + 16 * (t // RING + 1))
                    for c in range(4):
                        u = u0 + 2 * j + c // 2
                        pe.wait_ge(evac[u % 4], i * 2 + u // 4 + 1)
                        for m in range(KB):
                            ins = mm(pe, accb(m), wtile(t, c, m * P, P, D),
                                     big[:, bass.ds(i * (16 * S) + (4 * j + c) * S, S)], False, True)
                            if c == 0 and m == 0:
                                ins.then_inc(tile_begun, 1)
            mm(pe, acc[:, 3, :], zeros[0:1, 0:P], zeros[0:1, :], False, True).then_inc(acc_full, 1)
            u = u0 + 16
            pe.wait_ge(ada_step, 8 * ADA_PER * (st.at["ada"] + 1))
            pe_open(pe, u)
            for c in range(2 * ADA_PER):
                ins = mm(pe, wk(u, c, c + 1), att[:, c * P:c * P + P], R("ones", 0, 1))
            ins.then_inc(work_full, 1)

        def pe_postnorm(pe, st):
            pe_means(pe, st.at["unit"], st.at["sq"], R("mean1024"))
            if st.embeds:
                t = st.at["tile"]
                pe_tile(pe, t)
                for m in range(KB):
                    u = st.at["unit"] + 1 + m // 2
                    if m % 2 == 0:
                        pe_open(pe, u)
                    for k in range(2):
                        ins = mm(pe, wk(u, (m % 2) * S, (m % 2 + 1) * S), wtile(t, k, m * P, P, D),
                                 wtile(t, 0, 2 * D + k * S, S), k == 0, k == 1)
                        if m == 0 and k == 0:
                            ins.then_inc(tile_begun, 1)
                    if m % 2 == 1:
                        ins.then_inc(work_full, 1)

        def pe_ple(pe, st):
            wait_x(pe, st)
            for j in range(2):
                u = st.at["unit"] + 2 * j
                pe_feature_tile(pe, st.at["tile"] + j, (u, u + 1), lambda k: blk(xT, k))

        def pe_moe(pe, st):
            u0, t0 = st.at["unit"], st.at["tile"]
            pe.wait_ge(h_ready, 8 * st.at["h"])
            pe_open(pe, u0)
            for tt in range(2):
                o = wk(u0, tt * 32, tt * 32 + 20)
                for k in range(KB):
                    mm(pe, o, hT[:, k * S + tt * P:k * S + tt * P + P],
                       R("router", (st.layer * 8 + k) * 20, (st.layer * 8 + k) * 20 + 20), k == 0, False)
                ins = mm(pe, o, R("ones", rows=slice(0, 1)),
                         R("router_b", st.layer * 20, st.layer * 20 + 20, slice(0, 1)), False, True)
            ins.then_inc(work_full, 1)
            pe_clear_acc(pe)
            pe_open(pe, u0 + 1)
            pe.wait_ge(gates_ready, st.layer + 1)
            for tt in range(2):
                ins = pe_transpose(pe, wk(u0 + 1, tt * P, tt * P + P, slice(0, 16)), rt[:, 64 + 16 * tt:80 + 16 * tt])
            ins.then_inc(work_full, 1)
            wait_evacuated(pe, [u0 + 1])
            for e in range(NEXP):
                u = u0 + 2 + e // 2
                if e % 2 == 0:
                    pe_open(pe, u)
                ins = mm(pe, wk(u, (e % 2) * S, (e % 2 + 1) * S),
                         R("ident", e, e + 1, slice(0, 16)).broadcast_to([16, P]), gateT[:, :])
                if e % 2 == 1:
                    ins.then_inc(work_full, 1)
            ue = u0 + 10
            with pe.Fori(0, 4) as i:
                for e in range(4):
                    for w in range(2):
                        t = t0 + 3 * e + w
                        pe.wait_ge(landed[t % RING], i * 48 + 16 * (t // RING + 1))
                        for m in range(4):
                            u = ue + 4 * e + 2 * w + m // 2
                            if m % 2 == 0:
                                pe.wait_ge(evac[u % 4], i * 4 + u // 4)
                            for k in range(KB):
                                ins = mm(pe, wk(u, (m % 2) * S, (m % 2 + 1) * S), wtile(t, k, m * P), blk(hT, k),
                                         k == 0, k == KB - 1)
                                if m == 0 and k == 0:
                                    ins.then_inc(tile_begun, 1)
                            if m % 2 == 1:
                                ins.then_inc(work_full, 1)
                    t = t0 + 3 * e + 2
                    pe.wait_ge(landed[t % RING], i * 48 + 16 * (t // RING + 1))
                    for c in range(4):
                        u = ue + 4 * e + 2 + c // 2
                        pe.wait_ge(evac[u % 4], i * 4 + u // 4 + 1)
                        for m in range(KB):
                            ins = mm(pe, accb(m), wtile(t, c, m * P, P, D), blk(big, 8 + 4 * (e % 2) + c), False, True)
                            if c == 0 and m == 0:
                                ins.then_inc(tile_begun, 1)
            mm(pe, acc[:, 3, :], zeros[0:1, 0:P], zeros[0:1, :], False, True).then_inc(acc_full, 1)

        def act_full(act, u):
            act.wait_ge(work_full, u + 1)

        def act_out(act, u, dst, func=ACT.Copy, scale=1.0, a=0, b=512, rows=slice(0, P)):
            act_full(act, u)
            nc.scalar.activation(dst, wk(u, a, b, rows), func, scale=scale).then_inc(evac[u % 4], 1)

        def act_tables(act):
            nc.scalar.preload_act_table_set("natural_log_exp_and_others")

        def act_rstd(act, u):
            act_full(act, u)
            nc.scalar.activation(lnv[:, :], wk(u, 0, S), ACT.Ln, bias=R("eps")).then_inc(evac[u % 4], 1)
            act.wait_ge(evac[u % 4], u // 4 + 1)
            nc.scalar.activation(rstd[:, :], lnv[:, :], ACT.Exp, scale=-0.5).then_inc(rstd_ready, 1)

        def act_setup(act, st):
            act_out(act, 0, att[0:BIASH, 0:ROW], b=ROW, rows=slice(0, BIASH))
            act_out(act, 1, att[0:8, ROW:2 * ROW], b=ROW, rows=slice(0, 8))
            act_out(act, 2, cmp_bias[:, :], b=2 * NCMP * 16)
            nc.scalar.activation(silu_c[:, :], R("c2"), ACT.Silu).then_inc(setup_done, 1)
            act.wait_ge(dve_step, 5)
            nc.scalar.activation(lamv[:, 4:8], lamv[:, 0:4], ACT.Exp).then_inc(setup_done, 1)

        def act_norm(act, st):
            act_tables(act)
            for q in range(4):
                wait_x(act, st, q)
                nc.scalar.activation(blk(big, SQ + 2 * q, 2), blk(xT, 2 * q, 2), ACT.Square).then_inc(sq_ready, 1)
            act_rstd(act, st.at["unit"])

        def act_postnorm(act, st):
            act_tables(act)
            act.wait_ge(acc_full, st.at["acc"])
            for b in range(4):
                nc.scalar.activation(blk(big, SQ + 2 * b, 2), acc[:, b, :], ACT.Square).then_inc(sq_ready, 1)
            act_rstd(act, st.at["unit"])
            if st.embeds:
                for q in range(4):
                    act_out(act, st.at["unit"] + 1 + q, blk(big, 2 * q, 2))

        def act_mlp(act, st):
            u0 = st.at["unit"]
            with act.Fori(0, 2) as i:
                for j in range(8):
                    u = u0 + j
                    act.wait_ge(work_full, i * 8 + (u + 1))
                    nc.scalar.activation(blk(oT, 2 * (u % 4), 2), wk(u), ACT.Relu).then_inc(mlp_step, 1)

        def act_ple(act, st):
            for q in range(4):
                act_out(act, st.at["unit"] + q, blk(big, 8 + 2 * q, 2), ACT.Sigmoid)

        def act_exps(act, h, spans, done):
            for i, (slot, a, b, k) in enumerate(spans):
                ins = nc.scalar.activation(prob(slot, a, b), prob(slot, a, b), ACT.Exp,
                                           bias=stat(stat_max, h, k, k + 1),
                                           accum_out=None if done is None else stat(stat_sum, h, k, k + 1))
            ins.then_inc(exps_done, 1)

        def act_turned(act, f, h, pv0, pieces):
            if h >= 2:
                act.wait_ge(pv_full, pv0 + h - 1)
            act.wait_ge(tr_full, f + 1)
            for rows, a, b, to in pieces:
                ins = nc.scalar.activation(ptr(h % 2, to, to + b - a, rows), acc[rows, f % 2, a:b], ACT.Copy)
            ins.then_inc(tr_free, 1)

        def act_pv(act, n, rows, k):
            act.wait_ge(pv_full, n + 1)
            nc.scalar.activation(blk(oT, k, rows=rows), acc[rows, 2 + n % 2, 0:S], ACT.Copy).then_inc(pv_free, 1)

        allp = slice(0, P)

        def act_da(act, st):
            u = st.at["unit"]
            for q in range(4):
                act_out(act, u + q, blk(big, 2 * q, 2), scale=DH ** -0.5)
            for q in range(4):
                act_out(act, u + 4 + q, blk(big, 8 + 2 * q, 2))
            for q in range(4):
                act_out(act, u + 8 + q, pe_value(16, q % 2, (q // 2) * 512, 512))
            tr0, pv0, pr0 = st.at["tr"], st.at["pv"], st.at["head"]
            for s in range(8 + 2):
                if s < 8:
                    act.wait_ge(logits_ready, pr0 + s + 1)
                    act_exps(act, s, [(2 * (s % 2) + c, a, b, 2 * c + t)
                                      for c in range(2) for t, (a, b) in enumerate(((0, P), (P, ROW)))], True)
                if 0 <= s - 1 < 8:
                    act_turned(act, tr0 + s - 1, s - 1, pv0, [(allp, 0, ROW, 0)])
                if 0 <= s - 2 < 8:
                    act_pv(act, pv0 + s - 2, allp, s - 2)
            act.wait_ge(pv_free, pv0 + 8)
            for q in range(4):
                nc.scalar.activation(blk(big, SQ + 2 * q, 2), blk(oT, 2 * q, 2), ACT.Square).then_inc(sq_ready, 1)
            for q in range(4):
                v = u + 28 + q
                act_full(act, v)
                nc.scalar.activation(att[:, 512 * q:512 * q + 512], wk(v), ACT.Ln, bias=R("eps")).then_inc(evac[v % 4], 1)
                act.wait_ge(evac[v % 4], v // 4 + 1)
                nc.scalar.activation(att[:, 512 * q:512 * q + 512], att[:, 512 * q:512 * q + 512], ACT.Exp,
                                     scale=-0.5).then_inc(sub_rstd, 1)

        def act_nsa(act, st):
            u = st.at["unit"]
            for q in range(4):
                act_out(act, u + q, blk(big, 2 * q, 2), scale=DH ** -0.5)
            for q in range(4):
                act_out(act, u + 4 + q, blk(big, 8 + 2 * q, 2))
            for q in range(2):
                act_out(act, u + 8 + q, pe_value(16, q, 0, 512, 2))
            act_out(act, u + 10, gates_sb[:, :], ACT.Sigmoid, b=96)
            for kv in range(2):
                act_out(act, u + 11 + kv, gel[:, 120 * kv:120 * kv + 120], ACT.Gelu_apprx_tanh, b=120)
            act_out(act, u + 13, kcT[:, :], b=60)
            act_out(act, u + 14, vc[0:NCMP, :], b=256, rows=slice(0, NCMP))
            act_tables(act)
            tr0, pv0, pr0 = st.at["tr"], st.at["pv"], st.at["head"]
            for s in range(16 + 2):
                if s < 16:
                    a = 2 * (s % 2)
                    act.wait_ge(logits_ready, pr0 + s + 1)
                    act_exps(act, s, [(a, ROW, ROW + NCMP, 0), (a, ROW + 16, ROW + 16 + NCMP, 1), (a, 0, P, 2),
                                      (a, P, ROW, 3), (a + 1, 0, P, 4), (a + 1, P, ROW, 5)], True)
                if 0 <= s - 1 < 16:
                    for c in range(2):
                        act_turned(act, tr0 + 2 * (s - 1) + c, s - 1, pv0,
                                   [(allp, 0, ROW, 512 * c), (slice(0, NCMP), ROW, 512, 512 * c + ROW)])
                if 0 <= s - 2 < 16:
                    act_pv(act, pv0 + s - 2, half(s % 2), (s - 2) // 2)

        def act_heads(act, st, heads):
            tr0, pv0, pr0 = st.at["tr"], st.at["pv"], st.at["head"]
            for s in range(heads + 2):
                if s < heads:
                    act.wait_ge(logits_ready, pr0 + s + 1)
                    act_exps(act, s, [(s % 4, 0, P, 0), (s % 4, P, ROW, 1)], True)
                if 0 <= s - 1 < heads:
                    act_turned(act, tr0 + s - 1, s - 1, pv0, [(allp, 0, ROW, 0)])
                if 0 <= s - 2 < heads:
                    act_pv(act, pv0 + s - 2, half(s % 2), (s - 2) // 2)

        def act_fox(act, st):
            u = st.at["unit"]
            for q in range(4):
                act_out(act, u + q, blk(big, 2 * q, 2), scale=DH ** -0.5)
            for q in range(4):
                act_out(act, u + 4 + q, blk(big, 8 + 2 * q, 2))
            for q in range(4):
                act_out(act, u + 8 + q, pe_value(16, q % 2, (q // 2) * 512, 512))
            f, t = fox_f[:, 0:S], fox_f[:, S:2 * S]
            act.wait_ge(evac[(u + 12) % 4], (u + 12) // 4 + 1)
            nc.scalar.activation(t, f, ACT.Abs).then_inc(act_step, 1)
            act.wait_ge(act_step, 1)
            nc.scalar.activation(t, t, ACT.Exp, scale=-1.0).then_inc(act_step, 1)
            act.wait_ge(act_step, 2)
            nc.scalar.activation(t, t, ACT.Ln, bias=R("ones", 0, 1, slice(0, 16))).then_inc(act_step, 1)
            act_heads(act, st, 16)

        def act_ev(act, st):
            u = st.at["unit"]
            load_bias(act, copies2, 8, bias2_in)
            act.dma_start(biasT[:, 8 * ROW:8 * ROW + 1024], gmlp_gb).then_inc(bias2_in, 16)
            for q in range(2):
                act_out(act, u + q, blk(big, 2 * q, 2), scale=DH ** -0.5)
            for q in range(2):
                act_out(act, u + 2 + q, blk(big, 4 + 2 * q, 2))
            for q in range(2):
                act_out(act, u + 4 + q, pe_value(8, q, 0, 512, 2))
            for q in range(2):
                act_out(act, u + 6 + q, blk(big, 12 + 2 * q, 2), ACT.Gelu_apprx_tanh)
            for q in range(2):
                act_out(act, u + 8 + q, pe_value(16, q, 0, 512, 2), ACT.Gelu_apprx_tanh)
            act_tables(act)
            act.wait_ge(gated, 1)
            nc.scalar.activation(stat_sum[:, 92:94], stat_sum[:, 90:92], ACT.Ln, bias=R("eps")).then_inc(act_step, 1)
            act.wait_ge(act_step, 4)
            nc.scalar.activation(stat_sum[:, 94:96], stat_sum[:, 92:94], ACT.Exp, scale=-0.5).then_inc(act_step, 1)
            act_heads(act, st, 8)

        def act_od(act, st):
            u = st.at["unit"]
            for q in range(2):
                act_out(act, u + q, blk(big, 24 + 2 * q, 2))
            for q in range(2):
                act_out(act, u + 2 + q, blk(big, 28 + 2 * q, 2), ACT.Sigmoid)
            for q in range(2):
                act_out(act, u + 4 + q, blk(big, 2 * q, 2), scale=DH ** -0.5)
            for q in range(2):
                act_out(act, u + 6 + q, blk(big, 4 + 2 * q, 2))
            for q in range(2):
                act_out(act, u + 8 + q, pe_value(8, q, 0, 512, 2))
            pv0 = st.at["pv"]
            act_tables(act)
            for s in range(8 + 2):
                if s < 8:
                    t = big[:, 21 * S + (s % 2) * ROW:21 * S + (s % 2) * ROW + ROW]
                    act_full(act, u + 10 + s)
                    if s >= 2:
                        act.wait_ge(keep_ready, s - 1)
                    nc.scalar.activation(t, wk(u + 10 + s, 0, ROW), ACT.Abs).then_inc(act_step, 1)
                    act.wait_ge(act_step, 5 + 2 * s + 1)
                    nc.scalar.activation(t, t, ACT.Exp, scale=-1.0).then_inc(act_step, 1)
                    act.wait_ge(act_step, 5 + 2 * s + 2)
                    nc.scalar.activation(t, t, ACT.Ln, bias=R("ones", 0, 1)).then_inc(soft_ready, 1)
                if 0 <= s - 1 < 8:
                    h = s - 1
                    act.wait_ge(logits_ready, st.at["head"] + h + 1)
                    nc.scalar.activation(prob(2 * (h % 2), 0, ROW), prob(2 * (h % 2), 0, ROW), ACT.Exp).then_inc(exps_done, 1)
                if 0 <= s - 2 < 8:
                    act_pv(act, pv0 + s - 2, half(s % 2), 4 + (s - 2) // 2)
            v = u + 18
            act.wait_ge(evac[v % 4], v // 4 + 1)
            for k in range(4):
                nc.scalar.activation(blk(big, SQ + k), blk(big, 17 + k), ACT.Square).then_inc(sq_ready, 1)
            act_rstd(act, v + 1)
            act.wait_ge(conv_done, 2)
            for k in range(4):
                ins = nc.scalar.activation(blk(oT, k), blk(big, 17 + k), ACT.Silu, bias=R("convb", k, k + 1),
                                           scale=R("convg", k, k + 1))
            ins.then_inc(o_ready, 1)

        def act_moe(act, st):
            u0 = st.at["unit"]
            act.wait_ge(route_a, 2 * st.layer + 1)
            nc.scalar.activation(rt[:, 112:120], rt[:, 104:112], ACT.Exp).then_inc(route_b, 1)
            act.wait_ge(route_a, 2 * st.layer + 2)
            nc.scalar.activation(rt[:, 210:212], rt[:, 208:210], ACT.Exp).then_inc(route_b, 1)
            act_out(act, u0 + 1, gateT[:, :], b=S, rows=slice(0, 16))
            for q in range(8):
                act_out(act, u0 + 2 + q, att[:, 512 * q:512 * q + 512])
            ue = u0 + 10
            nc.scalar.preload_act_table_set("silu_and_others")
            with act.Fori(0, 4) as i:
                for e in range(4):
                    for q in range(2):
                        u = ue + 4 * e + q
                        act.wait_ge(work_full, i * 16 + (u + 1))
                        nc.scalar.activation(blk(big, 4 * (e % 2) + 2 * q, 2), wk(u), ACT.Silu).then_inc(evac[u % 4], 1)

        class Order:
            n = 0

            def step(self, ins):
                self.n += 1
                ins.then_inc(dve_step, 1)

            def settle(self, eng, back=0):
                eng.wait_ge(dve_step, self.n - back)

            def link(self, eng, ins):
                self.step(ins)
                self.settle(eng)

        own = Order()

        def dve_setup(v, st):
            own.link(v, v.memset(zeros[:, :], 0.0))
            v.wait_ge(loads, 16 * 2)
            for n in range(4):
                lo = SETUP["lam"][0] + 128 * n
                own.step(v.tensor_tensor_reduce(out=stat_max[:, 0:64], in0=big[:, lo:lo + 64], in1=big[:, lo + 64:lo + 128],
                                                scale=1.0, scalar=0.0, op0=ALU.mult, op1=ALU.add,
                                                accum_out=lamv[:, n:n + 1]))
                own.settle(v)
            v.wait_ge(work_full, 4)
            v.tensor_tensor(wsT[:, :].rearrange("p (g t) -> p g t", g=4), wk(3).rearrange("p (g t) -> p g t", g=4),
                            R("tri").unsqueeze(1).broadcast_to([P, 4, P]), ALU.mult).then_inc(evac[3], 1)
            v.wait_ge(setup_done, 2)
            for ia, i in enumerate((0, 3)):
                lam_init = 0.8 - 0.6 * math.exp(-0.3 * i)
                own.link(v, v.tensor_tensor(lamv[:, 12:13], lamv[:, 5 + 2 * ia:6 + 2 * ia], lamv[:, 4 + 2 * ia:5 + 2 * ia],
                                            ALU.subtract))
                own.step(v.tensor_scalar(lamv[:, 8 + ia:9 + ia], lamv[:, 12:13], -lam_init, None, ALU.add))
                own.link(v, v.tensor_scalar(lamv[:, 10 + ia:11 + ia], R("subln", ia, ia + 1), 1.0 - lam_init, None, ALU.mult))

        def dve_scaled(v, src, k, gain, dst):
            return v.scalar_tensor_tensor(blk(dst, k), src, gain, rstd[:, :], ALU.mult, ALU.mult)

        def dve_norm(v, st, which=None):
            n = st.layer * 4 + (0 if st.first else 2)
            v.wait_ge(rstd_ready, st.at["rstd"] + 1)
            for k in range(KB):
                dve_scaled(v, blk(xT, k), k, R("norm_g", n * 8 + k, n * 8 + k + 1), hT).then_inc(h_ready, 1)

        def dve_norm2(v, st):
            w = 0 if st.first else 1
            v.wait_ge(rstd_ready, st.at["rstd"] + 1)
            base = own.n
            for k in range(KB):
                c = (st.layer * 2 + w) * 8 + k
                own.step(dve_scaled(v, blk(xT, k), k, gain2[:, c:c + 1], oT))
            for k in range(KB):
                c = st.layer * 48 + 24 * w + k
                v.wait_ge(dve_step, base + k + 1)
                v.tensor_scalar(blk(hT, k), blk(oT, k), mod[:, c:c + 1], None, ALU.add).then_inc(h_ready, 1)

        def dve_postnorm(v, st):
            n = st.layer * 4 + (3 if st.embeds else 1)
            v.wait_ge(acc_full, st.at["acc"])
            v.wait_ge(rstd_ready, st.at["rstd"] + 1)
            base = own.n

            def add(q):
                v.wait_ge(dve_step, base + 2 * q + 2)
                v.tensor_tensor(blk(xT, 2 * q, 2), blk(xT, 2 * q, 2), blk(oT, 2 * q, 2), ALU.add).then_inc(x_ready, 1)

            for m in range(KB):
                own.step(dve_scaled(v, accb(m), m, R("norm_g", n * 8 + m, n * 8 + m + 1), oT))
                if m in (3, 5, 7):
                    add((m - 3) // 2)
            add(3)

        def dve_residual(v, st):
            c = st.layer * 48 + (16 if st.first else 40)
            v.wait_ge(acc_full, st.at["acc"])
            for m in range(KB):
                ins = v.scalar_tensor_tensor(blk(xT, m), accb(m), mod[:, c + m:c + m + 1], blk(xT, m), ALU.mult, ALU.add)
                if m % 2 == 1:
                    ins.then_inc(x_ready, 1)

        def dve_ple(v, st):
            u = st.at["unit"]
            base = own.n
            wait_evacuated(v, range(u - 4, u))
            for q in range(4):
                wait_evacuated(v, [u + q])
                own.step(v.tensor_tensor(blk(oT, 2 * q, 2), blk(big, 8 + 2 * q, 2), blk(big, 2 * q, 2), ALU.mult))
            for q in range(4):
                v.wait_ge(dve_step, base + q + 1)
                v.tensor_tensor(blk(xT, 2 * q, 2), blk(xT, 2 * q, 2), blk(oT, 2 * q, 2), ALU.add).then_inc(x_ready, 1)

        def dve_logits(v, u, slot, bias, h, k):
            v.wait_ge(work_full, u + 1)
            v.tensor_tensor(prob(slot, 0, ROW), wk(u, 0, ROW), bias, ALU.add).then_inc(evac[u % 4], 1)
            v.wait_ge(evac[u % 4], u // 4 + 1)
            v.tensor_reduce(stat(stat_max, h, k, k + 1), prob(slot, 0, P), AX.X, ALU.max, negate=True)
            return v.tensor_reduce(stat(stat_max, h, k + 1, k + 2), prob(slot, P, ROW), AX.X, ALU.max, negate=True)

        def dve_scale(v, slot, a, b, coef):
            return v.tensor_scalar(prob(slot, a, b), prob(slot, a, b), coef, None, ALU.mult)

        def dve_da(v, st):
            u0, tr0, pr0, ia = st.at["unit"] + 12, st.at["tr"], st.at["head"], (0 if st.layer == 0 else 1)
            if st.layer == 0:
                v.wait_ge(bias_in, 32)
            for s in range(8 + 1):
                if s < 8:
                    if s >= 2:
                        v.wait_ge(tr_full, tr0 + s - 1)
                    for c in range(2):
                        ins = dve_logits(v, u0 + 2 * s + c, 2 * (s % 2) + c, bias_of(2 * s + c), s, 2 * c)
                    ins.then_inc(logits_ready, 1)
                if s >= 1:
                    h, a = s - 1, 2 * ((s - 1) % 2)
                    v.wait_ge(exps_done, pr0 + h + 1)
                    own.link(v, v.reciprocal(stat(stat_coef, h, 0, 4), stat(stat_sum, h, 0, 4)))
                    own.link(v, v.tensor_scalar(stat(stat_coef, h, 2, 4), stat(stat_coef, h, 2, 4),
                                                lamv[:, 8 + ia:9 + ia], None, ALU.mult))
                    dve_scale(v, a + 1, 0, P, stat(stat_coef, h, 2, 3))
                    own.link(v, dve_scale(v, a + 1, P, ROW, stat(stat_coef, h, 3, 4)))
                    for t, (lo, hi) in enumerate(((0, P), (P, ROW))):
                        ins = v.scalar_tensor_tensor(prob(a, lo, hi), prob(a, lo, hi), stat(stat_coef, h, t, t + 1),
                                                     prob(a + 1, lo, hi), ALU.mult, ALU.add)
                    ins.then_inc(probs_ready, 1)
            for q in range(4):
                v.wait_ge(sub_rstd, st.at["sub"] + q + 1)
                ins = v.scalar_tensor_tensor(blk(oT, 2 * q, 2), blk(oT, 2 * q, 2), lamv[:, 10 + ia:11 + ia],
                                             att[:, 512 * q:512 * q + 512], ALU.mult, ALU.mult)
            ins.then_inc(o_ready, 1)

        def dve_nsa(v, st):
            u = st.at["unit"]
            z0 = 20 * S
            for kv in range(2):
                wait_evacuated(v, [u + 4 + kv])
                zk = big[:, z0 + kv * 960:z0 + kv * 960 + 960].rearrange("p (j g n) -> p j g n", j=16, g=4)
                for g in range(4):
                    src = blk(big, 8 + 2 * kv + g // 2, rows=half(g % 2)).rearrange("p (a j r) -> p r j a", a=16, j=8)
                    for r in range(2):
                        for jh in range(2):
                            ins = v.tensor_copy(zk[64 * r:64 * r + 64, 8 * jh:8 * jh + 8, g, :],
                                                src[:, r, :, jh:jh + NCMP])
                own.link(v, ins)
                zj = big[:, z0 + kv * 960:z0 + kv * 960 + 960].rearrange("p (j c) -> p j c", j=16)
                v.tensor_tensor(zj, zj, R("pe", 16 * kv, 16 * kv + 16).unsqueeze(2).broadcast_to([P, 16, 60]),
                                ALU.add).then_inc(z_ready, 1)
            wait_evacuated(v, [u + 10])
            u0, tr0, pr0 = u + 15, st.at["tr"], st.at["head"]
            cb = cmp_bias[:, :].rearrange("p (t n h) -> p h t n", t=2, n=NCMP)
            wait_evacuated(v, [2])
            gv = gates_sb[:, :].rearrange("p (t c) -> p c t", t=2)
            for s in range(16 + 1):
                if s < 16:
                    h, a, ua = first_head(s // 2, s % 2), 2 * (s % 2), u0 + 2 * s
                    if s >= 2:
                        v.wait_ge(tr_full, tr0 + 2 * (s - 1))
                    v.wait_ge(work_full, ua + 1)
                    cm = prob(a, ROW, ROW + 32).rearrange("p (t n) -> p t n", t=2)[:, :, 0:NCMP]
                    v.tensor_tensor(cm, wk(ua, ROW, ROW + 32).rearrange("p (t n) -> p t n", t=2)[:, :, 0:NCMP],
                                    cb[:, h], ALU.add)
                    dve_logits(v, ua, a, bias_of(h), s, 2)
                    v.tensor_reduce(stat(stat_max, s, 0, 2), cm, AX.X, ALU.max, negate=True)
                    dve_logits(v, ua + 1, a + 1, bias_of(h), s, 4).then_inc(logits_ready, 1)
                if s >= 1:
                    e, a = s - 1, 2 * ((s - 1) % 2)
                    h = first_head(e // 2, e % 2)
                    v.wait_ge(exps_done, pr0 + e + 1)
                    own.link(v, v.reciprocal(stat(stat_coef, e, 0, 6), stat(stat_sum, e, 0, 6)))
                    cf = stat(stat_coef, e, 0, 6).rearrange("p (b t) -> p b t", b=3)
                    own.link(v, v.tensor_tensor(cf, cf, gv[:, 3 * h:3 * h + 3, :], ALU.mult))
                    own.link(v, v.tensor_tensor(stat(stat_coef, e, 0, 1), stat(stat_coef, e, 0, 1), R("rowmask"), ALU.mult))
                    for slot, lo, hi, k in ((a, ROW, ROW + NCMP, 0), (a, ROW + 16, ROW + 16 + NCMP, 1), (a, 0, P, 2),
                                            (a, P, ROW, 3), (a + 1, 0, P, 4), (a + 1, P, ROW, 5)):
                        ins = dve_scale(v, slot, lo, hi, stat(stat_coef, e, k, k + 1))
                    ins.then_inc(probs_ready, 1)

        def dve_heads(v, st, u0, heads, bias, counts=False):
            tr0, pr0 = st.at["tr"], st.at["head"]
            for s in range(heads + 1):
                if s < heads:
                    if s >= 4:
                        v.wait_ge(tr_full, tr0 + s - 3)
                    dve_logits(v, u0 + s, s % 4, bias(s), s, 0).then_inc(logits_ready, 1)
                if s >= 1:
                    h = s - 1
                    v.wait_ge(exps_done, pr0 + h + 1)
                    if counts:
                        own.link(v, v.tensor_tensor(prob(h % 4, 0, ROW), prob(h % 4, 0, ROW), R("cnt"), ALU.mult))
                        v.tensor_reduce(stat(stat_sum, h, 2, 3), prob(h % 4, 0, P), AX.X, ALU.add)
                        own.link(v, v.tensor_reduce(stat(stat_sum, h, 3, 4), prob(h % 4, P, ROW), AX.X, ALU.add))
                    c = 2 if counts else 0
                    own.link(v, v.reciprocal(stat(stat_coef, h, 0, 2), stat(stat_sum, h, c, c + 2)))
                    dve_scale(v, h % 4, 0, P, stat(stat_coef, h, 0, 1))
                    dve_scale(v, h % 4, P, ROW, stat(stat_coef, h, 1, 2)).then_inc(probs_ready, 1)

        def dve_fox(v, st):
            u = st.at["unit"] + 12
            f, t, c, neg = (fox_f[:, i * S:(i + 1) * S] for i in range(4))
            v.wait_ge(work_full, u + 1)
            v.tensor_scalar(f, wk(u, 0, S, slice(0, 16)), R("fox_bf", rows=slice(0, 16)), None, ALU.add).then_inc(evac[u % 4], 1)
            v.wait_ge(act_step, 3)
            own.link(v, v.scalar_tensor_tensor(f, f, 0.0, t, ALU.min, ALU.subtract))
            own.link(v, v.memset(t, 1.0))
            own.link(v, v.tensor_tensor_scan(c, t, f, 0.0, ALU.mult, ALU.add))
            v.tensor_scalar(neg, c, -1.0, None, ALU.mult).then_inc(cum_ready, 1)
            dve_heads(v, st, u + 1, 16, lambda s: bias_of(16))

        def dve_ev(v, st):
            u = st.at["unit"]
            for n in range(2):
                wait_evacuated(v, [u + 8 + n])
                own.link(v, v.bn_stats(stat_coef[:, 80:86], pe_value(16, n, 0, 512, 2)))
                own.link(v, v.bn_aggr(stat_coef[:, 86 + 2 * n:88 + 2 * n], stat_coef[:, 80:86]))
            v.tensor_copy(stat_sum[:, 90:92], stat_coef[:, 86:90].rearrange("p (n c) -> p c n", n=2)[:, 1, :]).then_inc(gated, 1)
            v.wait_ge(act_step, 5)
            v.wait_ge(bias2_in, 48)
            gain, shift = biasT[:, 8 * ROW:8 * ROW + 512], biasT[:, 8 * ROW + 512:8 * ROW + 1024]
            for n in range(2):
                t = pe_value(16, n, 0, 512, 2)
                own.link(v, v.tensor_scalar(t, t, stat_coef[:, 86 + 2 * n:87 + 2 * n], stat_sum[:, 94 + n:95 + n],
                                            ALU.subtract, ALU.mult))
                own.link(v, v.tensor_tensor(t, t, gain, ALU.mult))
                ins = v.tensor_tensor(t, t, shift, ALU.add)
            ins.then_inc(z_ready, 1)
            dve_heads(v, st, u + 10, 8, lambda s: bias_of(s), counts=True)
            for i in range(2):
                w = u + 18 + i
                v.wait_ge(work_full, w + 1)
                v.tensor_tensor(blk(oT, 4 + 2 * i, 2), wk(w), blk(big, 12 + 2 * i, 2), ALU.mult).then_inc(evac[w % 4], 1)

        def dve_od(v, st):
            u = st.at["unit"]
            PAD = CONVW - 1
            W = PAD + S
            G = big[:, 12 * S:12 * S + 4 * W].rearrange("p (c t) -> p c t", c=4)
            own.step(v.memset(G[:, :, 0:PAD], 0.0))
            wait_evacuated(v, range(u, u + 4))
            own.link(v, v.tensor_tensor(G[:, :, PAD:W], blk(big, 24, 4).rearrange("p (c t) -> p c t", c=4),
                                        blk(big, 28, 4).rearrange("p (c t) -> p c t", c=4), ALU.mult))
            conv0 = []

            def taps(lo, hi):
                for j in range(lo, hi):
                    for c in range(4):
                        w, g, o = R("dw", c * CONVW + j, c * CONVW + j + 1), G[:, c, j:j + S], blk(big, 17 + c)
                        if j == 0:
                            own.step(v.tensor_scalar(o, g, w, R("dwb", c, c + 1), ALU.mult, ALU.add))
                        else:
                            v.wait_ge(dve_step, conv0[c])
                            own.step(v.scalar_tensor_tensor(o, g, w, o, ALU.mult, ALU.add))
                        conv0[c:c + 1] = [own.n]

            tr0, pr0 = st.at["tr"], st.at["head"]
            for s in range(8 + 1):
                if s < 8:
                    w, ls, keep = u + 10 + s, prob(2 * (s % 2), 0, ROW), prob(2 * (s % 2) + 1, 0, ROW)
                    t = big[:, 21 * S + (s % 2) * ROW:21 * S + (s % 2) * ROW + ROW]
                    v.wait_ge(soft_ready, s + 1)
                    if s >= 2:
                        v.wait_ge(tr_full, tr0 + s - 1)
                        v.wait_ge(probs_ready, pr0 + s - 1)
                    own.link(v, v.scalar_tensor_tensor(ls, wk(w, 0, ROW), 0.0, t, ALU.min, ALU.subtract))
                    v.tensor_tensor(keep, ls, wk(w, 0, ROW), ALU.subtract).then_inc(evac[w % 4], 1)
                    v.wait_ge(evac[w % 4], w // 4 + 1)
                    v.tensor_tensor(keep, keep, R("strict"), ALU.mult).then_inc(keep_ready, 1)
                if s >= 1:
                    h = s - 1
                    ls = prob(2 * (h % 2), 0, ROW)
                    v.wait_ge(tr_full, tr0 + h + 1)
                    v.tensor_tensor(ls, ls, acc[:, (tr0 + h) % 2, 0:ROW], ALU.add).then_inc(logits_ready, 1)
                taps(s * 4 if s < 8 else CONVW, min(s * 4 + 4, CONVW))
                if s >= 1:
                    h = s - 1
                    v.wait_ge(exps_done, pr0 + h + 1)
                    if h >= 2:
                        v.wait_ge(pv_full, st.at["pv"] + h - 1)
                    v.tensor_tensor(ptr(h % 2, 0, ROW), prob(2 * (h % 2), 0, ROW), R("strict"), ALU.mult).then_inc(probs_ready, 1)
            own.settle(v)
            v.sem_inc(conv_done, 1)
            conv, w = blk(big, 17, 4).rearrange("p (c t) -> p c t", c=4), u + 18
            v.wait_ge(work_full, w + 1)
            v.tensor_tensor(conv, conv, wk(w, 0, S).unsqueeze(1).broadcast_to([P, 4, S]), ALU.subtract).then_inc(evac[w % 4], 1)
            v.wait_ge(rstd_ready, st.at["rstd"] + 1)
            v.tensor_tensor(conv, conv, rstd[:, :].unsqueeze(1).broadcast_to([P, 4, S]), ALU.mult).then_inc(conv_done, 1)

        def dve_mlp(v, st):
            u0 = st.at["unit"]
            with v.Fori(0, 2) as i:
                for j in range(8):
                    u = u0 + j
                    v.wait_ge(mlp_step, i * 8 + (16 * st.at["ada"] + j + 1))
                    v.tensor_tensor(big[:, bass.ds(i * (16 * S) + 2 * j * S, 2 * S)], wk(u), blk(oT, 2 * (u % 4), 2),
                                    ALU.mult).then_inc(evac[u % 4], 1)
            a0, half_n = st.at["ada"] * ADA_PER, ADA_PER // 2
            if a0 == 0:
                v.wait_ge(setup_done, 2)
            with v.Fori(0, half_n) as i:
                for k in range(KB):
                    for b in range(2):
                        dst = att[:, bass.ds(i * (2 * ADAW) + b * ADAW, ADAW)]
                        w, c = ada_ring[:, b, k * ADAW:(k + 1) * ADAW], silu_c[:, k:k + 1]
                        if k == 0:
                            v.wait_ge(ada_landed[b], i * 16 + 16 * (a0 // 2 + 1))
                            v.tensor_scalar(dst, w, c, None, ALU.mult).then_inc(ada_step, 1)
                        else:
                            v.wait_ge(ada_step, i * 16 + (8 * a0 + 2 * (k - 1) + b + 1))
                            v.scalar_tensor_tensor(dst, w, c, dst, ALU.mult, ALU.add).then_inc(ada_step, 1)
            u = u0 + 16
            n = 2 * ADA_PER * st.at["ada"]
            v.wait_ge(work_full, u + 1)
            v.tensor_tensor(mod[:, n:n + 2 * ADA_PER], wk(u, 0, 2 * ADA_PER), R("b_ada", n, n + 2 * ADA_PER),
                            ALU.add).then_inc(evac[u % 4], 1)
            if st.layer == DEPTH - 1:
                v.wait_ge(evac[u % 4], u // 4 + 1)
                for c in range(4):
                    l, w = c // 2, c % 2
                    sc = l * 48 + 24 * w + 8
                    own.link(v, v.scalar_tensor_tensor(gain2[:, 8 * c:8 * c + 8], mod[:, sc:sc + 8], 1.0,
                                                       R("norm2_g2" if w else "norm1_g2", 8 * l, 8 * l + 8),
                                                       ALU.add, ALU.mult))

        def dve_moe(v, st):
            u0 = st.at["unit"]
            t2 = lambda a, n: rt[:, a:a + 2 * n].rearrange("p (t c) -> p t c", t=2)
            lg, rank = t2(0, 20), R("rank").unsqueeze(1).broadcast_to([P, 2, 4])
            over = lambda ap: ap.unsqueeze(2).broadcast_to([P, 2, 4])

            def first_of_max(vals, top, tmp, to):
                own.link(v, v.tensor_tensor(t2(tmp, 4), vals, over(rt[:, top:top + 2]), ALU.is_equal))
                own.link(v, v.tensor_tensor(t2(tmp, 4), t2(tmp, 4), rank, ALU.mult))
                own.link(v, v.tensor_reduce(rt[:, tmp + 8:tmp + 10], t2(tmp, 4), AX.X, ALU.max))
                own.link(v, v.tensor_tensor(t2(to, 4), t2(tmp, 4), over(rt[:, tmp + 8:tmp + 10]), ALU.is_equal))

            v.wait_ge(work_full, u0 + 1)
            v.tensor_copy(lg, wk(u0, 0, 64).rearrange("p (t c) -> p t c", t=2)[:, :, 0:20]).then_inc(evac[u0 % 4], 1)
            v.wait_ge(evac[u0 % 4], u0 // 4 + 1)
            own.link(v, v.tensor_reduce(rt[:, 100:102], lg[:, :, 0:4], AX.X, ALU.max))
            v.tensor_tensor(t2(104, 4), lg[:, :, 0:4], over(rt[:, 100:102]), ALU.subtract).then_inc(route_a, 1)
            first_of_max(lg[:, :, 0:4], 100, 240, 128)
            pr = rt[:, 136:168].rearrange("p (t g e) -> p t g e", t=2, g=4)
            for tt in range(2):
                own.step(v.tensor_tensor(pr[:, tt], lg[:, tt, 4:20].rearrange("p (g e) -> p g e", g=4),
                                         rt[:, 128 + 4 * tt:132 + 4 * tt].unsqueeze(2).broadcast_to([P, 4, 4]), ALU.mult))
            own.settle(v)
            own.link(v, v.tensor_reduce(t2(168, 4), pr.rearrange("p t g e -> p t e g"), AX.X, ALU.add))
            own.link(v, v.tensor_reduce(rt[:, 176:178], t2(168, 4), AX.X, ALU.max))
            first_of_max(t2(168, 4), 176, 252, 180)
            own.link(v, v.scalar_tensor_tensor(rt[:, 188:196], rt[:, 180:188], NEG, rt[:, 168:176], ALU.mult, ALU.add))
            own.link(v, v.tensor_reduce(rt[:, 196:198], t2(188, 4), AX.X, ALU.max))
            v.tensor_tensor(rt[:, 208:210], rt[:, 196:198], rt[:, 176:178], ALU.subtract).then_inc(route_a, 1)
            first_of_max(t2(188, 4), 196, 264, 200)
            v.wait_ge(route_b, 2 * st.layer + 2)
            own.step(v.tensor_reduce(rt[:, 216:218], t2(112, 4), AX.X, ALU.add))
            own.link(v, v.tensor_scalar(rt[:, 212:214], rt[:, 210:212], 1.0, None, ALU.add))
            own.step(v.reciprocal(rt[:, 216:218], rt[:, 216:218]))
            own.link(v, v.reciprocal(rt[:, 212:214], rt[:, 212:214]))
            own.link(v, v.tensor_tensor(rt[:, 212:214], rt[:, 212:214], rt[:, 216:218], ALU.mult))
            own.link(v, v.tensor_tensor(rt[:, 214:216], rt[:, 210:212], rt[:, 212:214], ALU.mult))
            own.step(v.tensor_tensor(t2(220, 4), t2(180, 4), over(rt[:, 212:214]), ALU.mult))
            own.link(v, v.tensor_tensor(t2(228, 4), t2(200, 4), over(rt[:, 214:216]), ALU.mult))
            own.link(v, v.tensor_tensor(t2(220, 4), t2(220, 4), t2(228, 4), ALU.add))
            gt = rt[:, 64:96].rearrange("p (t g e) -> p t g e", t=2, g=4)
            for tt in range(2):
                ins = v.tensor_tensor(gt[:, tt], rt[:, 128 + 4 * tt:132 + 4 * tt].unsqueeze(2).broadcast_to([P, 4, 4]),
                                      rt[:, 220 + 4 * tt:224 + 4 * tt].unsqueeze(1).broadcast_to([P, 4, 4]), ALU.mult)
            ins.then_inc(gates_ready, 1)
            wait_evacuated(v, range(u0 + 6, u0 + 10))
            ue, g0 = u0 + 10, 1 + 32 * st.layer
            with v.Fori(0, 4) as i:
                for e in range(4):
                    for q in range(2):
                        u = ue + 4 * e + q
                        v.wait_ge(evac[u % 4], i * 4 + (u // 4 + 1))
                        sg = blk(big, 4 * (e % 2) + 2 * q, 2).rearrange("p (c t) -> p c t", c=2)
                        gb = att[:, bass.ds(i * (4 * S) + e * S, S)].unsqueeze(1).broadcast_to([P, 2, S])
                        v.tensor_tensor(sg, sg, gb, ALU.mult).then_inc(gated, 1)
                    for q in range(2):
                        u = ue + 4 * e + 2 + q
                        v.wait_ge(gated, i * 8 + (g0 + 2 * e + q + 1))
                        v.wait_ge(work_full, i * 16 + (u + 1))
                        v.tensor_tensor(blk(big, 8 + 4 * (e % 2) + 2 * q, 2), wk(u), blk(big, 4 * (e % 2) + 2 * q, 2),
                                        ALU.mult).then_inc(evac[u % 4], 1)

        def dve_final(v, st):
            v.wait_ge(rstd_ready, st.at["rstd"] + 1)
            for k in range(KB):
                ins = dve_scaled(v, blk(xT, k), k, R("final_g2", k, k + 1), oT)
            ins.then_inc(o_ready, 1)

        for a, b in zip(plan, plan[1:] + [last]):
            a.first = b.kind in ("da", "nsa", "fox", "ev", "od")
            if a.kind == "residual":
                a.first = plan[plan.index(a) - 1].kind == "outproj"
        n_ada = ADA_PER * sum(st.kind == "mlp" for st in plan)

        def shifted(copies, heads, first, n):
            at = copies[0:1, 0, first:first + 1]
            return bass.AP(tensor=at.tensor, offset=at.offset, ap=[[ROW - 1, P], [P * ROW, heads], [1, n]])

        def load_bias(eng, copies, heads, done):
            bv = biasT[:, 0:heads * ROW].rearrange("p (h k) -> p h k", h=heads)
            eng.dma_start(bv[:, :, P:ROW], shifted(copies, heads, P - 1, S)).then_inc(done, 16)
            eng.dma_start(bv[:, :, 0:P], shifted(copies, heads, S - 1, P)).then_inc(done, 16)

        block = ctx.enter_context(nc.Block())

        @block.sync
        def _(sp):
            sp.dma_start(res[:, :], resident).then_inc(loads, 16)
            sp.dma_start(big[:, 0:SETUP_W], setup).then_inc(loads, 16)
            sp.dma_start(xT[:, :], x_in).then_inc(x_loaded, 16)
            for t in range(min(RING, n_tiles)):
                sp.dma_start(ring[:, t, :], stream[t]).then_inc(landed[t], 16)
            sp.wait_ge(evac[0], 1)
            sp.wait_ge(evac[1], 1)
            sp.dma_start(rows1, att[0:BIASH, 0:ROW]).then_inc(rows_out, 16)
            sp.dma_start(rows2, att[0:8, ROW:2 * ROW]).then_inc(rows_out, 16)
            sp.wait_ge(rows_out, 32)
            sp.dma_start(copies1, rows1.unsqueeze(1).broadcast_to([BIASH, P, ROW])).then_inc(rows_out, 16)
            sp.dma_start(copies2, rows2.unsqueeze(1).broadcast_to([8, P, ROW])).then_inc(rows_out, 16)
            sp.wait_ge(rows_out, 64)
            load_bias(sp, copies1, BIASH, bias_in)
            rounds = (n_tiles - RING) // RING
            if rounds > 0:
                with sp.Fori(0, rounds) as i:
                    for j in range(RING):
                        sp.wait_ge(tile_begun, i * RING + (j + 2))
                        sp.dma_start(ring[:, j, :], stream[bass.ds(i * RING + (RING + j), 1)].rearrange("a p n -> p (a n)")
                                     ).then_inc(landed[j], 16)
            for t in range(RING * (rounds + 1), n_tiles):
                sp.wait_ge(tile_begun, t - RING + 2)
                sp.dma_start(ring[:, t % RING, :], stream[t]).then_inc(landed[t % RING], 16)
            if last.kind == "final":
                sp.wait_ge(o_ready, last.at["o"] + 1)
                sp.dma_start(out, oT[:, :]).then_inc(stored, 16)
            else:
                sp.wait_ge(x_ready, 4 * n_x)
                sp.dma_start(out, xT[:, :]).then_inc(stored, 16)
            sp.wait_ge(stored, 16)

        @block.gpsimd
        def _(pool):
            for a in range(2):
                pool.dma_start(ada_ring[:, a, :], ada_stream[a]).then_inc(ada_landed[a], 16)
            if n_ada:
                with pool.Fori(0, n_ada // 2 - 1) as i:
                    pool.wait_ge(ada_step, i * 16 + 16)
                    for a in range(2):
                        pool.dma_start(ada_ring[:, a, :], ada_stream[bass.ds(i * 2 + (2 + a), 1)].rearrange("a p n -> p (a n)")
                                       ).then_inc(ada_landed[a], 16)

        @block.tensor
        def _(pe):
            steps = {"setup": pe_setup, "norm": pe_norm, "norm2": pe_norm, "final": pe_norm, "da": pe_da, "nsa": pe_nsa,
                     "fox": pe_fox, "ev": pe_ev, "od": pe_od, "mlp": pe_mlp, "postnorm": pe_postnorm, "ple": pe_ple,
                     "moe": pe_moe}
            for before, st in zip([None] + plan, plan):
                if st.kind == "outproj":
                    pe_outproj(pe, st, before)
                elif st.kind in steps:
                    steps[st.kind](pe, st)

        @block.scalar
        def _(act):
            act.wait_ge(loads, 16 * 2)
            steps = {"setup": act_setup, "norm": act_norm, "norm2": act_norm, "final": act_norm, "da": act_da,
                     "nsa": act_nsa, "fox": act_fox, "ev": act_ev, "od": act_od, "postnorm": act_postnorm,
                     "mlp": act_mlp, "ple": act_ple, "moe": act_moe}
            for st in plan:
                if st.kind in steps:
                    steps[st.kind](act, st)

        @block.vector
        def _(v):
            steps = {"setup": dve_setup, "norm": dve_norm, "norm2": dve_norm2, "final": dve_final, "da": dve_da,
                     "nsa": dve_nsa, "fox": dve_fox, "ev": dve_ev, "od": dve_od, "mlp": dve_mlp,
                     "postnorm": dve_postnorm, "ple": dve_ple, "residual": dve_residual, "moe": dve_moe}
            for st in plan:
                if st.kind in steps:
                    steps[st.kind](v, st)


def columns(v):
    v = np.asarray(v)
    return np.ascontiguousarray(v.reshape(-1, P).T)


def pack(a):
    f = np.float32
    q = {k: np.asarray(v) for k, v in a.items()}
    res = np.zeros((P, RES_W), f)

    def put(name, value, at=0):
        value = np.asarray(value)
        lo = RES[name][0] + at
        res[0:value.shape[0], lo:lo + value.shape[1]] = value

    i, j = np.arange(P)[:, None], np.arange(P)[None, :]
    put("ident", (i == j).astype(f))
    for name, n in (("mean1024", 1024), ("mean128", 128), ("mean512", 512), ("ones", 1)):
        put(name, np.full((P, P), 1.0 / n, f))
    put("later", (i > j).astype(f))
    put("tri", (j >= i).astype(f))
    kq = np.arange(S)[None, :]
    put("strict", np.concatenate([(i < kq), (i < j)], 1).astype(f))
    d = (i + P) - np.arange(S)[None, :]
    cnt = branch_count(d).astype(f)
    put("cnt", np.concatenate([cnt[:, P:], cnt], 1))
    put("rowmask", (i >= 31).astype(f))
    put("rank", np.tile(np.array([[4, 3, 2, 1]], f), (P, 1)))
    put("eps", np.full((P, 1), EPS, f))
    put("norm_g", columns(q["norm_g"].reshape(-1)))
    put("norm1_g2", columns(q["norm1_g_2"].reshape(-1)))
    put("norm2_g2", columns(q["norm2_g_2"].reshape(-1)))
    put("final_g2", columns(q["final_norm_g_2"]))
    put("c2", columns(q["c_2"][0]))
    put("b_ada", columns(q["b_ada_2"].reshape(-1)))
    put("subln", columns(q["da_subln"].reshape(-1)))
    put("dw", q["od_w_dw_2"][0].reshape(CONVW, 4, P).transpose(2, 1, 0).reshape(P, -1))
    put("dwb", columns(q["od_b_dw_2"][0]))
    put("convg", columns(q["od_conv_ln_g_2"][0]))
    put("convb", columns(q["od_conv_ln_b_2"][0]))
    w = q["nsa_w_in"][0]
    put("nsa_gate", w[:, 2560:].reshape(8, P, 48).transpose(1, 0, 2).reshape(P, -1))
    w2 = q["nsa_cmp_w2"][0].reshape(2, 2, P, DH).transpose(0, 2, 1, 3)
    put("cmp_w2k", np.concatenate([w2[0], w2[0]], 2).reshape(P, -1))
    put("cmp_w2v", w2[1].reshape(P, -1))
    put("pe", q["nsa_cmp_pe"][0].reshape(2, 16, P).transpose(2, 0, 1).reshape(P, -1))
    put("fox_wf", q["fox_w_in"][0][:, 3 * D:].reshape(8, P, 16).transpose(1, 0, 2).reshape(P, -1))
    put("fox_bf", q["fox_b_f"][0][:, None])
    for l in range(DEPTH2):
        r = np.concatenate([q["moe_w_group_2"][l], q["moe_w_router_2"][l].transpose(1, 0, 2).reshape(D, 16)], 1)
        put("router", r.reshape(8, P, 20).transpose(1, 0, 2).reshape(P, -1), 160 * l)
        put("router_b", np.concatenate([q["moe_b_group_2"][l], q["moe_b_router_2"][l].reshape(-1)])[None], 20 * l)
    put("gmlp_bs", q["ev_b_s_2"][0].reshape(1, -1))

    setup = np.zeros((P, SETUP_W), f)

    def put_setup(name, value):
        value = np.asarray(value)
        lo = SETUP[name][0]
        setup[0:value.shape[0], lo:lo + value.shape[1]] = value

    back = 255 - np.arange(ROW)
    put_setup("oh1", one_hot_rows(bucket_first, back, back >= 0))
    put_setup("oh2", one_hot_rows(bucket_second, back, branch_count(back) > 0))
    ahead = np.arange(512) - 256
    put_setup("ohf", one_hot_rows(bucket_first, ahead, ahead >= 0))
    put_setup("rel1", np.concatenate([np.concatenate([q["rel_bias"], np.zeros((32, 1), f)], 1), np.ones((1, 17), f)], 0))
    put_setup("rel2", np.concatenate([q["rel_bias_2"], np.ones((1, 8), f)], 0))
    put_setup("lam", np.broadcast_to(q["da_lambda"].reshape(1, 512), (P, 512)))
    put_setup("w_s", q["ev_w_s_2"][0].transpose(1, 0, 2).reshape(P, 512))
    gb = np.broadcast_to(np.concatenate([q["ev_gmlp_ln_g_2"][0], q["ev_gmlp_ln_b_2"][0]])[None], (P, 1024))

    tiles = np.zeros((NTILES, P, TILE), f)
    at = [0]

    def rows_of(w, kb):
        return w.reshape(kb, P, -1).transpose(1, 0, 2).reshape(P, -1)

    def tile(block):
        tiles[at[0], :, 0:block.shape[1]] = block
        at[0] += 1

    def wide(w):
        for c in range(0, w.shape[1], COLS):
            tile(rows_of(w[:, c:c + COLS], KB))

    def tall(w):
        for r in range(0, w.shape[0], 512):
            tile(rows_of(w[r:r + 512], 4))

    heads = [first_head(n // 2, n % 2) for n in range(16)]
    ia = 0
    for l in range(DEPTH):
        if KINDS[l] == "da":
            wide(q["da_w_in"][ia])
            wide(q["da_w_out"][ia])
            ia += 1
        elif KINDS[l] == "nsa":
            wq = w[:, 0:D].reshape(D, 16, DH)[:, heads].reshape(D, D)
            kc, vcm, ks, vs, kw, vw = (w[:, D + 256 * n:D + 256 * n + 256] for n in range(6))
            wide(np.concatenate([wq, kc, vcm, ks, kw, vs, vw], 1))
            for kv in range(2):
                tile(rows_of(q["nsa_cmp_w1"][0, kv], 16))
            wide(q["nsa_w_out"][0].reshape(16, DH, D)[heads].reshape(D, D))
        else:
            wide(q["fox_w_in"][0][:, 0:3 * D])
            wide(q["fox_w_out"][0])
        wide(q["mlp_w1"][l])
        tall(q["mlp_w2"][l])
        tile(np.concatenate([rows_of(q["ple_w"][l], 2), rows_of(q["p"][l, 0].T, 2)], 1))
        wide(q["ple_gate_w"][l])
    for l in range(DEPTH2):
        wide(q["ev_w_in_2"][0] if l == 0 else q["od_w_in_2"][0])
        wide(q["ev_w_out_2"][0] if l == 0 else q["od_w_out_2"][0])
        for e in range(NEXP):
            wide(q["moe_w_gate_2"][l, e])
            wide(q["moe_w_up_2"][l, e])
            tall(q["moe_w_down_2"][l, e])
    ada = q["w_ada_2"].reshape(2, 8, P, 24, ADAW).transpose(0, 3, 2, 1, 4).reshape(NADA, P, KB * ADAW)
    return {
        "x_in": np.ascontiguousarray(q["x"][0].reshape(S, 8, P).transpose(2, 1, 0).reshape(P, -1)),
        "resident": res, "setup": setup, "gmlp_gb": np.ascontiguousarray(gb), "stream": tiles,
        "ada_stream": np.ascontiguousarray(ada),
    }


def kernel(**inputs):
    import concourse.bacc as bacc
    from concourse.bass_utils import run_bass_kernel_spmd

    nc = bacc.Bacc("TRN2", target_bir_lowering=False, num_devices=1)
    arrays = pack(inputs)
    args = [nc.dram_tensor("in_" + n, a.shape, mybir.dt.from_np(a.dtype), kind="ExternalInput").ap() for n, a in arrays.items()]
    out = nc.dram_tensor("out", (P, KB * S), F32, kind="ExternalOutput").ap()
    build(nc, *args, out)
    r = run_bass_kernel_spmd(nc, [{"in_" + n: a for n, a in arrays.items()}], core_ids=[0])
    got = r.results[0]["out"]
    return got.reshape(P, KB, S).transpose(2, 1, 0).reshape(1, S, D)
```
